# Optimizing a Trainium2 kernel written in Bass

```python
import math
import jax
import jax.numpy as jnp
from jax import lax
import numpy as np

D_MODEL = 2048
BATCH = 1
SEQ = 1024
DEPTH = 1
DEC_BATCH = 1
DEC_SEQ = 32
PAST_LEN = 512

CHUNK = 64
HEAD_DIM = 64
MIX_WIDTH = D_MODEL
N_HEADS_TOTAL = MIX_WIDTH // HEAD_DIM
H_A = 3 * N_HEADS_TOTAL // 8
H_B = 3 * N_HEADS_TOTAL // 8
H_B_KV = H_B // 3
H_C = N_HEADS_TOTAL - H_A - H_B
W_A = H_A * HEAD_DIM
W_B = H_B * HEAD_DIM
KV_B = H_B_KV * HEAD_DIM
W_C = H_C * HEAD_DIM
SB_BLOCK = 128
WINDOW = 128
B_PREV_CHUNKS = WINDOW // CHUNK
C_PREV_CHUNKS = 8
C_REACH = C_PREV_CHUNKS * CHUNK
REL_CLIP = 128
NORM_EPS = 1e-6
MASK_VALUE = -1e30
SPLIT_SIZES = (W_A, W_A, W_A, W_A, W_B, KV_B, KV_B, W_B, W_C, W_C, W_C, W_C)
D_IN = sum(SPLIT_SIZES)

kernel_name = 'hybrid_streaming_sb_swa_chunkband_step'

def rms_norm(x, gain):
    xf = x.astype(jnp.float32)
    y = xf * lax.rsqrt(jnp.mean(xf * xf, axis=-1, keepdims=True) + NORM_EPS)
    return (y * gain.astype(jnp.float32)).astype(x.dtype)

def heads(x, n):
    return x.reshape(x.shape[:-1] + (n, HEAD_DIM))

def split_projection(h, w_in):
    p = jnp.einsum('btd,de->bte', h, w_in)
    offsets = [int(o) for o in np.cumsum(SPLIT_SIZES)[:-1]]
    return jnp.split(p, offsets, axis=-1)

def alibi_slopes(n):
    def geometric(m):
        start = 2.0 ** (-8.0 / m)
        return [start ** (i + 1) for i in range(m)]
    if n & (n - 1) == 0:
        vals = geometric(n)
    else:
        c = 2 ** int(math.floor(math.log2(n)))
        vals = geometric(c) + geometric(2 * c)[0::2][: n - c]
    return jnp.asarray(vals, dtype=jnp.float32)

def alibi_bias(slopes, q_pos, k_pos):
    dist = jnp.abs(q_pos[:, :, None] - k_pos[:, None, :]).astype(jnp.float32)
    return -slopes[None, :, None, None] * dist[:, None]

def rel_pos_bias(table, q_pos, k_pos):
    idx = jnp.clip(q_pos[:, :, None] - k_pos[:, None, :], -REL_CLIP, REL_CLIP) + REL_CLIP
    return jnp.moveaxis(table.astype(jnp.float32)[:, idx], 0, 1)

def stick_breaking(q, k, v, q_pos, k_pos):
    z = jnp.einsum('bqhd,bkhd->bhqk', q, k, preferred_element_type=jnp.float32) * (HEAD_DIM ** -0.5)
    earlier = k_pos[None, :] < q_pos[:, None]
    log_beta = jax.nn.log_sigmoid(z)
    log_keep = jnp.where(earlier, jax.nn.log_sigmoid(-z), 0.0)
    log_later = lax.cumsum(log_keep, axis=3, reverse=True) - log_keep
    weights = jnp.where(earlier, jnp.exp(log_beta + log_later), 0.0)
    return jnp.einsum('bhqk,bkhd->bqhd', weights.astype(v.dtype), v)

def band_attention(q, k, v, q_pos, k_pos, n_prev, bias, sinks):
    b, g, tq, hq, dh = q.shape
    tk, hkv = k.shape[2], k.shape[3]
    rep = hq // hkv
    qg = q.reshape(b, g, tq, hkv, rep, dh)
    s = jnp.einsum('bgqkrd,bgskd->bgkrqs', qg, k, preferred_element_type=jnp.float32)
    s = s.reshape(b, g, hq, tq, tk) * (dh ** -0.5) + bias[None]
    dc = q_pos[:, :, None] // CHUNK - k_pos[:, None, :] // CHUNK
    visible = (dc >= 0) & (dc <= n_prev) & (k_pos[:, None, :] >= 0)
    s = jnp.where(visible[None, :, None], s, MASK_VALUE)
    if sinks is not None:
        sink = jnp.broadcast_to(sinks.astype(jnp.float32)[None, None, :, None, None], (b, g, hq, tq, 1))
        p = jax.nn.softmax(jnp.concatenate([s, sink], axis=-1), axis=-1)[..., :-1]
    else:
        p = jax.nn.softmax(s, axis=-1)
    p = p.reshape(b, g, hkv, rep, tq, tk).astype(v.dtype)
    o = jnp.einsum('bgkrqs,bgskd->bgqkrd', p, v)
    return o.reshape(b, g, tq, hq, dh)

def chunk_band(x, n_prev):
    b, t, h, dh = x.shape
    nc = t // CHUNK
    xc = x.reshape(b, nc, CHUNK, h, dh)
    xp = jnp.pad(xc, ((0, 0), (n_prev, 0), (0, 0), (0, 0), (0, 0)))
    return jnp.concatenate([xp[:, j:j + nc] for j in range(n_prev + 1)], axis=2)

def band_positions(nc, n_prev):
    q_pos = jnp.arange(nc * CHUNK).reshape(nc, CHUNK)
    k_pos = (jnp.arange(nc)[:, None] - n_prev) * CHUNK + jnp.arange((n_prev + 1) * CHUNK)[None]
    return q_pos, k_pos

def last_rows(x, n):
    t = x.shape[1]
    if t >= n:
        return x[:, t - n:]
    return jnp.pad(x, ((0, 0), (n - t, 0), (0, 0), (0, 0)))

def gated_concat(oa, ga, ob, gb, oc, gc):
    return jnp.concatenate([oa * jax.nn.silu(ga), ob * jax.nn.silu(gb), oc * jax.nn.silu(gc)], axis=-1)

def mixers_prompt(h, w_in, sinks, rel_table, slopes):
    b, t, _ = h.shape
    qa, ka, va, ga, qb, kb, vb, gb, qc, kc, vc, gc = split_projection(h, w_in)
    qa, ka, va = heads(qa, H_A), heads(ka, H_A), heads(va, H_A)
    kb, vb = heads(kb, H_B_KV), heads(vb, H_B_KV)
    kc, vc = heads(kc, H_C), heads(vc, H_C)
    pos = jnp.arange(t)
    blocks = []
    for i in range(t // SB_BLOCK):
        lo, hi = i * SB_BLOCK, (i + 1) * SB_BLOCK
        blocks.append(stick_breaking(qa[:, lo:hi], ka[:, :hi], va[:, :hi], pos[lo:hi], pos[:hi]))
    oa = jnp.concatenate(blocks, axis=1).reshape(b, t, W_A)
    nc = t // CHUNK
    qpos_b, kpos_b = band_positions(nc, B_PREV_CHUNKS)
    ob = band_attention(heads(qb, H_B).reshape(b, nc, CHUNK, H_B, HEAD_DIM),
                        chunk_band(kb, B_PREV_CHUNKS), chunk_band(vb, B_PREV_CHUNKS),
                        qpos_b, kpos_b, B_PREV_CHUNKS, alibi_bias(slopes, qpos_b, kpos_b), sinks).reshape(b, t, W_B)
    qpos_c, kpos_c = band_positions(nc, C_PREV_CHUNKS)
    oc = band_attention(heads(qc, H_C).reshape(b, nc, CHUNK, H_C, HEAD_DIM),
                        chunk_band(kc, C_PREV_CHUNKS), chunk_band(vc, C_PREV_CHUNKS),
                        qpos_c, kpos_c, C_PREV_CHUNKS, rel_pos_bias(rel_table, qpos_c, kpos_c), None).reshape(b, t, W_C)
    mixed = gated_concat(oa, ga, ob, gb, oc, gc)
    lb, lc = min(WINDOW, PAST_LEN), min(C_REACH, PAST_LEN)
    return mixed, (ka, va, last_rows(kb, lb), last_rows(vb, lb), last_rows(kc, lc), last_rows(vc, lc))

def mixers_sample(h, ca_k, ca_v, cb_k, cb_v, cc_k, cc_v, w_in, sinks, rel_table, slopes):
    b, t, _ = h.shape
    past = ca_k.shape[1]
    qa, ka, va, ga, qb, kb, vb, gb, qc, kc, vc, gc = split_projection(h, w_in)
    qa, ka, va = heads(qa, H_A), heads(ka, H_A), heads(va, H_A)
    kb, vb = heads(kb, H_B_KV), heads(vb, H_B_KV)
    kc, vc = heads(kc, H_C), heads(vc, H_C)
    q_pos = past + jnp.arange(t)
    ka_all = jnp.concatenate([ca_k, ka], axis=1)
    va_all = jnp.concatenate([ca_v, va], axis=1)
    oa = stick_breaking(qa, ka_all, va_all, q_pos, jnp.arange(past + t)).reshape(b, t, W_A)
    qpos = q_pos[None]
    lb = cb_k.shape[1]
    kb_all = jnp.concatenate([cb_k, kb], axis=1)
    vb_all = jnp.concatenate([cb_v, vb], axis=1)
    kpos_b = jnp.concatenate([past - lb + jnp.arange(lb), q_pos])[None]
    ob = band_attention(heads(qb, H_B)[:, None], kb_all[:, None], vb_all[:, None], qpos, kpos_b,
                        B_PREV_CHUNKS, alibi_bias(slopes, qpos, kpos_b), sinks).reshape(b, t, W_B)
    lc = cc_k.shape[1]
    kc_all = jnp.concatenate([cc_k, kc], axis=1)
    vc_all = jnp.concatenate([cc_v, vc], axis=1)
    kpos_c = jnp.concatenate([past - lc + jnp.arange(lc), q_pos])[None]
    oc = band_attention(heads(qc, H_C)[:, None], kc_all[:, None], vc_all[:, None], qpos, kpos_c,
                        C_PREV_CHUNKS, rel_pos_bias(rel_table, qpos, kpos_c), None).reshape(b, t, W_C)
    mixed = gated_concat(oa, ga, ob, gb, oc, gc)
    return mixed, (ka, va, kb_all[:, -lb:], vb_all[:, -lb:], kc_all[:, -lc:], vc_all[:, -lc:])

def setup_inputs(seed: int = 0) -> dict:
    key = jax.random.key(seed)
    ks = jax.random.split(key, 14)
    lb, lc = min(WINDOW, PAST_LEN), min(C_REACH, PAST_LEN)
    f32 = jnp.float32
    return {
        'x_prompt': jax.random.normal(ks[0], (BATCH, SEQ, D_MODEL), f32),
        'x_sample': jax.random.normal(ks[1], (DEC_BATCH, DEC_SEQ, D_MODEL), f32),
        'cache_a_k': jax.random.normal(ks[2], (DEPTH, DEC_BATCH, PAST_LEN, H_A, HEAD_DIM), f32),
        'cache_a_v': jax.random.normal(ks[3], (DEPTH, DEC_BATCH, PAST_LEN, H_A, HEAD_DIM), f32),
        'cache_b_k': jax.random.normal(ks[4], (DEPTH, DEC_BATCH, lb, H_B_KV, HEAD_DIM), f32),
        'cache_b_v': jax.random.normal(ks[5], (DEPTH, DEC_BATCH, lb, H_B_KV, HEAD_DIM), f32),
        'cache_c_k': jax.random.normal(ks[6], (DEPTH, DEC_BATCH, lc, H_C, HEAD_DIM), f32),
        'cache_c_v': jax.random.normal(ks[7], (DEPTH, DEC_BATCH, lc, H_C, HEAD_DIM), f32),
        'norm_pre': 1.0 + 0.1 * jax.random.normal(ks[8], (DEPTH, D_MODEL), f32),
        'norm_post': 1.0 + 0.1 * jax.random.normal(ks[9], (DEPTH, D_MODEL), f32),
        'w_in': jax.random.normal(ks[10], (DEPTH, D_MODEL, D_IN), f32) * D_MODEL ** -0.5,
        'w_out': jax.random.normal(ks[11], (DEPTH, MIX_WIDTH, D_MODEL), f32) * MIX_WIDTH ** -0.5,
        'attn_sinks': 0.5 * jax.random.normal(ks[12], (DEPTH, H_B), f32),
        'rel_bias': 0.1 * jax.random.normal(ks[13], (DEPTH, H_C, 2 * REL_CLIP + 1), f32),
    }

def reference(x_prompt, x_sample, cache_a_k, cache_a_v, cache_b_k, cache_b_v, cache_c_k, cache_c_v,
              norm_pre, norm_post, w_in, w_out, attn_sinks, rel_bias):
    slopes = alibi_slopes(H_B)
    y_prompt, y_sample = x_prompt, x_sample
    p_states, s_states = [], []
    for l in range(DEPTH):
        hp = rms_norm(y_prompt, norm_pre[l])
        mp, st_p = mixers_prompt(hp, w_in[l], attn_sinks[l], rel_bias[l], slopes)
        y_prompt = y_prompt + rms_norm(jnp.einsum('btm,md->btd', mp, w_out[l]), norm_post[l])
        hs = rms_norm(y_sample, norm_pre[l])
        ms, st_s = mixers_sample(hs, cache_a_k[l], cache_a_v[l], cache_b_k[l], cache_b_v[l],
                                 cache_c_k[l], cache_c_v[l], w_in[l], attn_sinks[l], rel_bias[l], slopes)
        y_sample = y_sample + rms_norm(jnp.einsum('btm,md->btd', ms, w_out[l]), norm_post[l])
        p_states.append(st_p)
        s_states.append(st_s)
    new_a_k_prompt = jnp.stack([st[0] for st in p_states])
    new_a_v_prompt = jnp.stack([st[1] for st in p_states])
    new_b_k_prompt = jnp.stack([st[2] for st in p_states])
    new_b_v_prompt = jnp.stack([st[3] for st in p_states])
    new_c_k_prompt = jnp.stack([st[4] for st in p_states])
    new_c_v_prompt = jnp.stack([st[5] for st in p_states])
    new_a_k_sample = jnp.stack([st[0] for st in s_states])
    new_a_v_sample = jnp.stack([st[1] for st in s_states])
    new_b_k_sample = jnp.stack([st[2] for st in s_states])
    new_b_v_sample = jnp.stack([st[3] for st in s_states])
    new_c_k_sample = jnp.stack([st[4] for st in s_states])
    new_c_v_sample = jnp.stack([st[5] for st in s_states])
    return (y_prompt, y_sample,
            new_a_k_prompt, new_a_v_prompt, new_a_k_sample, new_a_v_sample,
            new_b_k_prompt, new_b_v_prompt, new_b_k_sample, new_b_v_sample,
            new_c_k_prompt, new_c_v_prompt, new_c_k_sample, new_c_v_sample)


_drawn_inputs = setup_inputs


def setup_inputs(seed=0):
    import zlib

    import numpy as np

    out = dict(_drawn_inputs(seed))
    spreads = {}
    factors = {'attn_sinks': 6.947, 'rel_bias': 7.318}
    for name, (base, spread) in spreads.items():
        noise = np.random.default_rng([zlib.crc32(name.encode()), seed]).standard_normal(out[name].shape)
        drawn = base * np.exp(spread * noise) if base else spread * noise
        out[name] = jnp.asarray(drawn.astype(out[name].dtype))
    for name, factor in factors.items():
        out[name] = (out[name] * factor).astype(out[name].dtype)
    return out
```

```python
from contextlib import ExitStack

import concourse.bass as bass
import numpy as np
from concourse import mybir

F32, F32R, BF16 = mybir.dt.float32, mybir.dt.float32r, mybir.dt.bfloat16
ALU, ACT, AX = mybir.AluOpType, mybir.ActivationFunctionType, mybir.AxisListType

P = 128
D = 2048
KT = D // P
SEQ, DEC, PAST = 1024, 32, 512
TOK = SEQ + DEC
GROUPS = 3
GN = TOK // GROUPS
DH = 64
CHUNK = 64
H_A, H_B, H_BKV, H_C = 12, 12, 4, 8
W_A, W_B, KV_B, W_C = H_A * DH, H_B * DH, H_BKV * DH, H_C * DH
NA, NB, NC = H_A // 2, H_BKV // 2, H_C // 2
REP = H_B // H_BKV
WINDOW, CLIP = 128, 128
EPS = 1e-6
SCALE = DH ** -0.5
NEG = -1e30
E_CAP = 2.0 ** 60

A_Q, A_K, A_V, A_G = 0, W_A, 2 * W_A, 3 * W_A
B_Q = 4 * W_A
B_K, B_V, B_G = B_Q + W_B, B_Q + W_B + KV_B, B_Q + W_B + 2 * KV_B
C_Q = B_G + W_B
C_K, C_V, C_G = C_Q + W_C, C_Q + 2 * W_C, C_Q + 3 * W_C

PIECE = 512
RING = 4
TILES = 4 * NA + (2 + 2 * REP) * NB + 4 * NC
PAIRS = NA + REP * NB + NC
TT = SEQ // P
TR = 7
GATE_PARTS = 8
BQ = 4 * P


def a_steps():
    steps = []
    for j in range(SEQ // BQ):
        for h in range(2):
            for pos, i in enumerate(range(4 * j + 3, -1, -1)):
                steps.append((j, h, i, max(0, P * (i - 4 * j)), pos))
    return steps


A_STEPS = a_steps()
NSTEP_A = len(A_STEPS) + 2
LAST = [i == 0 for _, _, i, _, _ in A_STEPS]
R_BEFORE = [sum(not x for x in LAST[:t]) for t in range(len(LAST) + 1)]
BAND = [(m, h) for m in range(TT + 1) for h in range(2)]
NSTEP_B = len(BAND)
ENDS_A, ENDS_B = (7, 23, 25), (7, 15, 17)


def build(nc, x_prompt, x_sample, cache_a_k, cache_a_v, cache_b_k, cache_b_v, cache_c_k, cache_c_v,
          norm_pre, norm_post, w_in, w_out, attn_sinks, rel_bias, alibi,
          y_prompt, y_sample, ak_p, av_p, ak_s, av_s, bk_p, bv_p, bk_s, bv_s, ck_p, cv_p, ck_s, cv_s):
    ctx = ExitStack()
    with ctx:
        def sb(name, shape, dt=F32):
            return ctx.enter_context(nc.sbuf_tensor(name, shape, dt))

        def sem(name):
            return ctx.enter_context(nc.semaphore(name))

        act_hi_t = sb("act_hi", [P, KT * TOK + P - DEC], F32R)
        act_lo_t = sb("act_lo", [P, KT * TOK + P - DEC], F32R)
        act_hi = act_hi_t[:, 0:KT * TOK].rearrange("p (k t) -> p k t", k=KT)
        act_lo = act_lo_t[:, 0:KT * TOK].rearrange("p (k t) -> p k t", k=KT)
        w_raw = sb("w_raw", [P, RING, PIECE])
        w_hi = sb("w_hi", [P, RING, PIECE], F32R)
        w_lo = sb("w_lo", [P, RING, PIECE], F32R)
        arena = sb("arena", [P, 11616])
        at = [0]

        def cut(n):
            at[0] += n
            return arena[:, at[0] - n:at[0]]

        kT = cut(TOK + P - DEC)
        qT, gT, oT = cut(TOK), cut(TOK), cut(TOK)
        v_nat = cut(9 * P).rearrange("p (b c) -> p b c", b=9)
        kc = cut(4 * P).rearrange("p (b c) -> p b c", b=4)
        vc = cut(4 * P).rearrange("p (b c) -> p b c", b=4)
        kcT = cut(4 * P)
        work0 = at[0]
        work = cut(4608)
        k_nat = work[:, 0:9 * P].rearrange("p (b c) -> p b c", b=9)
        e_buf = [work[:, 512 * i:512 * i + 512] for i in (0, 1)]
        sp_buf = [work[:, 512 * i:512 * i + 512] for i in (2, 3)]
        r_buf = [work[:, 512 * i:512 * i + 512] for i in (4, 5)]
        wt_buf = [work[:, 512 * i:512 * i + 512] for i in (6, 7)]
        s_buf = [work[:, 640 * i:640 * i + 640] for i in (0, 1, 2)]
        pT_buf = [work[:, 640 * i:640 * i + 640] for i in (3, 4)]
        bias = work[:, 3200:4480].rearrange("p (h c) -> p h c", h=2)
        x_t = [arena[:, 1152 + D * i:1152 + D * i + D] for i in (0, 1)]
        pre_gain = arena[:, 1152 + 2 * D:1152 + 3 * D]
        y = arena[:, 0:5 * D].rearrange("p (t c) -> p t c", t=5)
        post_gain = [arena[:, 5 * D + 512 * i:5 * D + 512 * i + 512] for i in (0, 1)]
        x_res = [[arena[:, 4 * D + 1024 * i:4 * D + 1024 * i + 1024] for i in (0, 1)],
                 [w_raw[:, 2 * i:2 * i + 2, :].rearrange("p a b -> p (a b)") for i in (0, 1)]]

        mask_c = sb("mask_c", [P, 640])
        ident = sb("ident", [P, P])
        neg_tri = sb("neg_tri", [P, P])
        neg_ones = sb("neg_ones", [P, P])
        ident_b = sb("ident_b", [P, P], BF16)
        mask_b = sb("mask_b", [P, P], BF16)
        small = sb("small", [P, 170])
        ssq, var = small[:, 0:9], small[:, 9:18]
        neg_max, row_sum, rden = (small[:, 20 + 18 * i:38 + 18 * i] for i in range(3))
        sink_in, neg_sink = small[:, 92:94], small[:, 94:96]
        ssq_y = small[:, 96:132]
        std_x, std_y, newton = small[:, 141:143], small[:, 160:169], small[:, 144:145]
        var_y = small[:, 132:141]
        tab = work[0:H_C, 2048:2048 + 2 * CLIP + 1]
        ext = work[0:H_C, 2560:2560 + 384]

        ps = ctx.enter_context(nc.psum_tensor("ps", [P, 8 * 512], F32))

        def bank(b, n=512, r=P, c=0):
            return ps[0:r, 512 * b + c:512 * b + c + n]

        X = 3
        O_BANK = 7

        mixed_d = nc.dram_tensor("mixed_scratch", (D, TOK), F32, kind="Internal").ap()
        ext_d = nc.dram_tensor("rel_ext", (H_C, 384), F32, kind="Internal")
        toep_d = nc.dram_tensor("rel_toeplitz", (H_C, P, 2 * P), F32, kind="Internal").ap()

        x_in = [sem("x_in0"), sem("x_in1")]
        gain_in = sem("gain_in")
        x_sq, x_var, x_std, x_rstd, x_norm = (sem(n) for n in ("x_sq", "x_var", "x_std", "x_rstd", "x_norm"))
        xt_done, x_hi, x_lo = sem("xt_done"), sem("x_hi"), sem("x_lo")
        consts = sem("consts")
        rel_in, ext_made, ext_out, toep_out = sem("rel_in"), sem("ext_made"), sem("ext_out"), sem("toep_out")
        raw_in = [sem(f"raw_in{i}") for i in range(RING)]
        hi_made, lo_made, piece_used = sem("hi_made"), sem("lo_made"), sem("piece_used")
        proj_done, proj_out = sem("proj_done"), sem("proj_out")
        tr_done, tr_out = sem("tr_done"), sem("tr_out")
        kc_in, vc_in = sem("kc_in"), sem("vc_in")
        k_stored, v_stored, cache_moved = sem("k_stored"), sem("v_stored"), sem("cache_moved")
        z_ready, e_ready, e_capped, l_ready = sem("z_ready"), sem("e_ready"), sem("e_capped"), sem("l_ready")
        sp_ready, r_ready, t_done, w_ready, pv_done = (sem(n) for n in ("sp_ready", "r_ready", "t_done", "w_ready", "pv_done"))
        gate_exp, gate_made = sem("gate_exp"), sem("gate_made")
        o_done, mix_made, mix_stored = sem("o_done"), sem("mix_made"), sem("mix_stored")
        bias_in, bias_made = sem("bias_in"), sem("bias_made")
        s_ready, s_biased, p_exp, den_made, p_normed = (sem(n) for n in ("s_ready", "s_biased", "p_exp", "den_made", "p_normed"))
        pt_done, pt_out, bpv_done = sem("pt_done"), sem("pt_out"), sem("bpv_done")
        mixed_in = [sem(f"mixed_in{i}") for i in range(4)]
        mx_hi, mx_lo = sem("mx_hi"), sem("mx_lo")
        post_in = [sem("post_in0"), sem("post_in1")]
        y_done, y_sq, y_out = sem("y_done"), sem("y_sq"), sem("y_out")
        yv_sum, yv_var, yv_std, yv_rstd = (sem(n) for n in ("yv_sum", "yv_var", "yv_std", "yv_rstd"))
        res_in = [sem("res_in0"), sem("res_in1")]
        fin_made, y_stored = sem("fin_made"), sem("y_stored")

        w_in_v = w_in[0].rearrange("(k p) c -> p k c", p=P)
        w_out_v = w_out[0].rearrange("(k p) c -> p k c", p=P)
        CONSTS = 9

        passed = {e.engine: sem(f"passed_{n}") for n, e in (("pe", nc.tensor), ("dve", nc.vector), ("pool", nc.gpsimd))}

        def a_tile(i, n):
            return 4 * i + n

        def b_tile(b, n):
            return 4 * NA + (2 + 2 * REP) * b + n

        def c_tile(c, n):
            return 4 * NA + (2 + 2 * REP) * NB + 4 * c + n

        def stored(kind, i, r=0):
            if kind == "a":
                return 16 * i + 1
            if kind == "b":
                return 16 * NA + 32 * (REP * i + r) + 1
            return 16 * NA + 32 * REP * NB + 16 * i + 1

        MIX_ALL = 16 * NA + 32 * REP * NB + 16 * NC + 1

        PARTS = (("a", NA), ("b", NB), ("c", NC))

        def numbers(kind, i):
            if kind == "a":
                return 4 * i, i, i
            if kind == "b":
                return b_tile(i, 0), NA + REP * i, NA + i
            return c_tile(i, 0), NA + REP * NB + i, NA + NB + i

        TOKSETS = ((0, 1, 2, 3), (4, 5, 6, 7, 8))
        NCH = D // PIECE
        P3 = 4 * TILES

        block = ctx.enter_context(nc.Block())

        def wait_apart(eng, s, value):
            eng.wait_ge(s, value)
            eng.sem_inc(passed[eng.engine], 1)

        @block.sync
        def _(sp):
            def cols(T, base, halves=None):
                for q in range(4):
                    if not (isinstance(T, int) and T == 0):
                        sp.wait_ge(lo_made, 4 * T + q - 3)
                    dst = w_raw[:, q, :].rearrange("p (k c) -> p k c", k=4)
                    if halves is None:
                        sp.dma_start(dst, w_in_v[:, 4 * q:4 * q + 4, bass.ds(base, P)]).then_inc(raw_in[q], 16)
                    else:
                        for s, b in enumerate(halves):
                            sp.dma_start(dst[:, :, 64 * s:64 * s + 64],
                                         w_in_v[:, 4 * q:4 * q + 4, bass.ds(b, 64)]).then_inc(raw_in[q], 8 * 2)

            def caches(kind, i):
                _, pair, kv = numbers(kind, i)
                if not isinstance(i, int) or kind != "a" or i > 0:
                    sp.wait_ge(o_done, 3 * pair)
                nb = 1 if kind == "b" else 4
                ck, cv = {"a": (cache_a_k, cache_a_v), "b": (cache_b_k, cache_b_v), "c": (cache_c_k, cache_c_v)}[kind]
                for cache, dst, s in ((ck, kc, kc_in), (cv, vc, vc_in)):
                    src = cache[0, 0].rearrange("(b p) h d -> p b (h d)", p=P)
                    sp.dma_start(dst[:, 0:nb, :], src[:, :, bass.ds(P * i, P)]).then_inc(s, 16)

            def store(kind, i, which):
                kvn = numbers(kind, i)[2]
                prompt, sample = {"a": ((ak_p, ak_s), (av_p, av_s)), "b": ((bk_p, bk_s), (bv_p, bv_s)),
                                  "c": ((ck_p, ck_s), (cv_p, cv_s))}[kind][which]
                src, s = ((k_nat, k_stored), (v_nat, v_stored))[which]
                keep = {"a": SEQ, "b": WINDOW, "c": PAST}[kind]
                total = {"a": DEC, "b": WINDOW, "c": PAST}[kind]
                sp.wait_ge(tr_out, TR * kvn + (3, TR)[which])
                sp.dma_start(prompt[0, 0].rearrange("(b p) h d -> p b (h d)", p=P)[:, :, bass.ds(P * i, P)],
                             src[:, (SEQ - keep) // P:8, :]).then_inc(s, 16)
                sp.dma_start(sample[0, 0].rearrange("t h d -> t (h d)")[total - DEC:total, bass.ds(P * i, P)],
                             src[0:DEC, 8, :]).then_inc(s, 16)

            def store_mixed(pair, rows):
                sp.wait_ge(mix_made, 3 * pair + 4)
                n = P // len(rows)
                for s, row in enumerate(rows):
                    sp.dma_start(mixed_d[bass.ds(row, n), :], oT[n * s:n * s + n, :]).then_inc(mix_stored, 16)

            def unit_a(i, nxt):
                caches("a", i)
                cols(a_tile(i, 1), A_V + P * i)
                cols(a_tile(i, 2), A_Q + P * i)
                cols(a_tile(i, 3), A_G + P * i)
                store("a", i, 0)
                nxt()
                store("a", i, 1)
                store_mixed(i, [P * i])

            sp.dma_start(x_t[0], x_prompt[0, 0:P, :]).then_inc(x_in[0], 16)
            sp.dma_start(x_t[1], x_prompt[0, P:2 * P, :]).then_inc(x_in[1], 16)
            sp.dma_start(pre_gain, norm_pre[0].partition_broadcast(P)).then_inc(gain_in, 16)
            cols(0, A_K)
            with sp.Fori(0, TT // 2 - 1) as i:
                for s in (0, 1):
                    sp.wait_ge(xt_done, 4 * (2 * i + s) + 4)
                    sp.dma_start(x_t[s], x_prompt[0, bass.ds(P * (2 * i + 2 + s), P), :]).then_inc(x_in[s], 16)
            sp.wait_ge(xt_done, 4 * (TT - 2) + 4)
            sp.dma_start(x_t[0][0:DEC, :], x_sample[0]).then_inc(x_in[0], 16)
            sp.wait_ge(ext_made, 2)
            sp.dma_start(ext_d.ap(), ext).then_inc(ext_out, 16)
            sp.wait_ge(ext_out, 16)
            sp.dma_start(toep_d, bass.AP(ext_d, P - 1, [[384, H_C], [-1, P], [1, 2 * P]])).then_inc(toep_out, 16)
            sp.wait_ge(x_lo, 4 * (TT + 1))

            unit_a(0, lambda: cols(a_tile(1, 0), A_K + P))
            with sp.Fori(1, NA - 1) as i:
                unit_a(i, lambda: cols(a_tile(i + 1, 0), A_K + P * i + P))
            unit_a(NA - 1, lambda: cols(b_tile(0, 0), B_K))

            for b in range(NB):
                caches("b", b)
                cols(b_tile(b, 1), B_V + P * b)
                for r in range(REP):
                    h0 = 2 * REP * b + r
                    pair = NA + REP * b + r
                    cols(b_tile(b, 2 + 2 * r), None, [B_Q + DH * h0, B_Q + DH * (h0 + REP)])
                    if r == 1:
                        store("b", b, 1)
                    if r:
                        store_mixed(pair - 1, [W_A + DH * (h0 - 1), W_A + DH * (h0 - 1 + REP)])
                    sp.wait_ge(o_done, 3 * pair)
                    for s in (0, 1):
                        sp.dma_start(bias[:, s, 0:2 * P], alibi[h0 + REP * s]).then_inc(bias_in, 16)
                        sp.dma_start(sink_in[:, s:s + 1],
                                     attn_sinks[0, h0 + REP * s:h0 + REP * s + 1].partition_broadcast(P)).then_inc(bias_in, 16)
                    cols(b_tile(b, 3 + 2 * r), None, [B_G + DH * h0, B_G + DH * (h0 + REP)])
                    if r == 0:
                        store("b", b, 0)
                if b + 1 < NB:
                    cols(b_tile(b + 1, 0), B_K + P * (b + 1))
                else:
                    cols(c_tile(0, 0), C_K)
                store_mixed(pair, [W_A + DH * h0, W_A + DH * (h0 + REP)])

            def unit_c(c, nxt):
                caches("c", c)
                cols(c_tile(c, 1), C_V + P * c)
                cols(c_tile(c, 2), C_Q + P * c)
                for s in (0, 1):
                    sp.dma_start(bias[:, s, 3 * P:5 * P], toep_d[bass.ds(2 * c + s, 1)].rearrange("o q k -> (o q) k")).then_inc(bias_in, 16)
                cols(c_tile(c, 3), C_G + P * c)
                store("c", c, 0)
                if nxt:
                    cols(c_tile(c + 1, 0), C_K + P * c + P)
                else:
                    for k in range(RING):
                        out_piece(0, 0, k)
                store("c", c, 1)
                if not nxt:
                    sp.wait_ge(proj_done, 3 * TILES)
                    sp.wait_ge(mix_stored, MIX_ALL - 16)
                    for j in range(4):
                        mixed_load(4 * j, min(4 * j + 4, KT - 1), mixed_in[j])
                store_mixed(NA + REP * NB + c, [W_A + W_B + P * c])

            def out_piece(g, n, k):
                pc = P3 + KT * NCH * g + KT * n + k
                sp.wait_ge(lo_made, pc - 3)
                sp.dma_start(w_raw[:, k % RING, :], w_out_v[:, k, bass.ds(PIECE * n, PIECE)]).then_inc(raw_in[k % RING], 16)

            def mixed_load(k0, k1, s):
                sp.dma_start(act_lo[:, k0:k1, :].bitcast(F32),
                             mixed_d[P * k0:P * k1, :].rearrange("(k p) t -> p k t", p=P)).then_inc(s, 16)

            sp.wait_ge(toep_out, 16)
            with sp.Fori(0, NC - 1) as c:
                unit_c(c, True)
            unit_c(NC - 1, False)

            sp.wait_ge(mix_stored, MIX_ALL)
            mixed_load(KT - 1, KT, mixed_in[3])

            def gain_chunk(g, n):
                if not (g == 0 and n < 2):
                    done = (0, len(TOKSETS[0]) * NCH)[g]
                    prev = NCH * g + n - 2
                    sp.wait_ge(y_out, out_count(prev + 1))
                sp.dma_start(post_gain[n % 2], norm_post[0, PIECE * n:PIECE * n + PIECE].partition_broadcast(P)).then_inc(post_in[n % 2], 16)

            def out_count(chunks):
                return sum(len(TOKSETS[c // NCH]) for c in range(chunks))

            e = 0
            for g in range(2):
                for n in range(NCH):
                    gain_chunk(g, n)
                    for k in range(RING, KT):
                        out_piece(g, n, k)
                    if n + 1 < NCH:
                        for k in range(RING):
                            out_piece(g, n + 1, k)
                    elif g == 0:
                        for k in range(RING):
                            out_piece(1, 0, k)
                if g == 1:
                    sp.wait_ge(lo_made, P3 + 2 * KT * NCH)
                for tt in TOKSETS[g]:
                    for half in (0, 1):
                        if e >= 2:
                            sp.wait_ge(fin_made, e - 1)
                        c = slice(1024 * half, 1024 * half + 1024)
                        if tt < TT:
                            sp.dma_start(x_res[g][half], x_prompt[0, P * tt:P * tt + P, c]).then_inc(res_in[half], 16)
                        else:
                            sp.dma_start(x_res[g][half][0:DEC, :], x_sample[0, :, c]).then_inc(res_in[half], 16)
                        e += 1

        @block.tensor
        def _(pe):
            mm = nc.tensor.matmul

            def wait_for(s, value, apart):
                if apart:
                    wait_apart(pe, s, value)
                else:
                    pe.wait_ge(s, value)

            def x_tile(t, s, rows):
                for g in range(4):
                    b = (0, 1, 2, 7)[g]
                    pe.wait_ge(x_norm, t + 1)
                    if not (isinstance(t, int) and t == 0):
                        pe.wait_ge(x_lo, 4 * t + g - 3)
                    for c in range(4):
                        last = nc.tensor.transpose(ps[:, 512 * b + rows * c:512 * b + rows * c + rows],
                                                   x_t[s][0:rows, P * (4 * g + c):P * (4 * g + c) + P],
                                                   ident[0:rows, 0:rows])
                    last.then_inc(xt_done, 1)

            pe.wait_ge(consts, CONSTS)
            x_tile(0, 0, P)
            x_tile(1, 1, P)
            with pe.Fori(1, TT // 2) as i:
                x_tile(2 * i, 0, P)
                x_tile(2 * i + 1, 1, P)
            x_tile(TT, 0, DEC)
            pe.wait_ge(x_lo, 4 * (TT + 1))

            def project(T):
                for q in range(4):
                    pe.wait_ge(lo_made, 4 * T + q + 1)
                    for g in range(GROUPS):
                        if q == 0:
                            pe.wait_ge(proj_out, 3 * T + g + 1)
                        for kk in range(4):
                            k = 4 * q + kk
                            wh, wl = w_hi[:, q, P * kk:P * kk + P], w_lo[:, q, P * kk:P * kk + P]
                            ah, al = act_hi[:, k, GN * g:GN * g + GN], act_lo[:, k, GN * g:GN * g + GN]
                            mm(bank(g, GN), wh, ah, start=(k == 0), stop=False)
                            mm(bank(g, GN), wh, al, start=False, stop=False)
                            last = mm(bank(g, GN), wl, ah, start=False, stop=(k == KT - 1))
                        if q == 3:
                            last.then_inc(proj_done, 1)
                    if q < 3:
                        last.then_inc(piece_used, 1)

            def turn(src, b, blocks, rows, cols, sem_at):
                for n, c in enumerate(blocks):
                    last = nc.tensor.transpose(ps[0:cols, 512 * b + P * n:512 * b + P * n + P if rows == P else 512 * b + P * n + rows],
                                               src(c), ident[0:rows, 0:rows])
                last.then_inc(tr_done, 1)

            def turn_rows(src, kvn, lot):
                for g in range(3):
                    b = X + g
                    if lot == 4:
                        pe.wait_ge(tr_out, TR * kvn + g + 1)
                    if g < 2:
                        for n in range(4):
                            t = 4 * g + n
                            last = nc.tensor.transpose(bank(b, P, P, P * n), src[:, P * t:P * t + P], ident[:, :])
                    else:
                        last = nc.tensor.transpose(bank(b, P, DEC), src[:, SEQ:TOK], ident[:, :])
                    last.then_inc(tr_done, 1)

            def turn_cache(kvn, nb):
                pe.wait_ge(kc_in, 16 * (kvn + 1))
                for n in range(nb):
                    last = nc.tensor.transpose(bank(X + 3, P, P, P * n), kc[:, n, :], ident[:, :])
                last.then_inc(tr_done, 1)

            def stick_breaking(i, T, pair, kvn):
                pe.wait_ge(proj_out, 3 * (T + 2) + 6)
                pe.wait_ge(tr_out, TR * kvn + TR)
                base = NSTEP_A * i

                def scores(t):
                    zb = X + t % 4
                    if t >= 4:
                        pe.wait_ge(w_ready, base + t - 3)
                    if t < len(A_STEPS):
                        j, h, kt, c0, _ = A_STEPS[t]
                        hp = slice(DH * h, DH * h + DH)
                        last = mm(bank(zb, BQ - c0, P, c0), kT[hp, P * kt:P * kt + P], qT[hp, BQ * j + c0:BQ * j + BQ],
                                  start=True, stop=False, skip_group_check=True)
                        if kt >= 4 * j:
                            last = mm(bank(zb, P, P, c0), ident_b[:, :], mask_b[:, :], start=False, stop=False,
                                      skip_group_check=True)
                    else:
                        h = t - len(A_STEPS)
                        hp = slice(DH * h, DH * h + DH)
                        for blk in range(5):
                            keys = kcT[hp, P * blk:P * blk + P] if blk < 4 else kT[hp, SEQ:SEQ + P]
                            mm(bank(zb, DEC, P, DEC * blk), keys, qT[hp, SEQ:TOK], start=(blk == 0), stop=False,
                               skip_group_check=True)
                        last = mm(bank(zb, DEC, P, DEC * 4), ident_b[:, :], mask_b[:, 0:DEC],
                                  start=False, stop=False, skip_group_check=True)
                    last.then_inc(z_ready, 1)

                def suffix(t):
                    zb = X + t % 4
                    pe.wait_ge(sp_ready, base + t + 1)
                    sp_t = sp_buf[t % 2]
                    if t < len(A_STEPS):
                        j, h, kt, c0, pos = A_STEPS[t]
                        last = mm(bank(zb, BQ - c0, P, c0), neg_tri[:, :], sp_t[:, c0:BQ], start=False, stop=(pos == 0),
                                  skip_group_check=True)
                        if pos:
                            pe.wait_ge(r_ready, R_BEFORE[-1] * i + R_BEFORE[t])
                            c1 = A_STEPS[t - 1][3]
                            last = mm(bank(zb, BQ - c1, P, c1), neg_ones[:, :], r_buf[pos % 2][:, c1:BQ],
                                      start=False, stop=True, skip_group_check=True)
                    else:
                        mm(bank(zb, 5 * DEC), neg_tri[:, :], sp_t[:, 0:5 * DEC], start=False, stop=False,
                           skip_group_check=True)
                        for blk in range(1, 5):
                            later = sp_t[:, DEC * blk:DEC * blk + DEC].unsqueeze(1).broadcast_to([P, blk, DEC])
                            last = mm(bank(zb, DEC * blk), neg_ones[:, :], later, start=False, stop=(blk == 4),
                                      skip_group_check=True)
                    last.then_inc(t_done, 1)

                def values(t):
                    pe.wait_ge(w_ready, base + t + 1)
                    wt = wt_buf[t % 2]
                    if t in (0, 8, 24):
                        pe.wait_ge(mix_made, 3 * pair + (0, 8, 24).index(t) + 1)
                    if t < len(A_STEPS):
                        j, h, kt, c0, pos = A_STEPS[t]
                        hp = slice(DH * h, DH * h + DH)
                        last = mm(ps[hp, 512 * O_BANK + c0:512 * O_BANK + BQ], v_nat[:, kt, hp], wt[:, c0:BQ],
                                  start=(pos == 0), stop=(kt == 0), skip_group_check=True)
                    else:
                        h = t - len(A_STEPS)
                        hp = slice(DH * h, DH * h + DH)
                        for blk in range(5):
                            rows = P if blk < 4 else DEC
                            v = vc[:, blk, hp] if blk < 4 else v_nat[0:DEC, 8, hp]
                            last = mm(ps[hp, 512 * O_BANK:512 * O_BANK + DEC], v, wt[0:rows, DEC * blk:DEC * blk + DEC],
                                      start=(blk == 0), stop=(blk == 4), skip_group_check=True)
                    last.then_inc(o_done if t in ENDS_A else pv_done, 1)

                pe.wait_ge(vc_in, 16 * (kvn + 1))
                pe.wait_ge(proj_out, 3 * (T + 3) + 6)
                for t in range(NSTEP_A + 3):
                    if t < NSTEP_A:
                        scores(t)
                    if 0 <= t - 2 < NSTEP_A:
                        suffix(t - 2)
                    if 0 <= t - 3:
                        values(t - 3)

            def band(n, nb, T, pair, kvn):
                pe.wait_ge(proj_out, 3 * T + 6)
                pe.wait_ge(tr_out, TR * kvn + TR)
                pe.wait_ge(vc_in, 16 * (kvn + 1))
                pe.wait_ge(proj_out, 3 * T + 9)
                base = NSTEP_B * n
                nc_keys = P if nb == 2 else 4 * P

                def keys_of(m):
                    return P * min(m + 1, nb)

                def scores(t):
                    m, h = BAND[t]
                    hp = slice(DH * h, DH * h + DH)
                    sb_ = X + 2 * (t % 2)
                    if t >= 2:
                        wait_for(s_biased, base + t - 1, m == TT)
                    if m < TT:
                        nk = keys_of(m)
                        k0 = P * (m + 1) - nk
                        for c in range(0, nk, 512):
                            w = min(512, nk - c)
                            last = mm(bank(sb_, w, P, c), qT[hp, P * m:P * m + P], kT[hp, k0 + c:k0 + c + w],
                                      start=True, stop=True, skip_group_check=True)
                    else:
                        mm(bank(sb_, nc_keys, DEC), qT[hp, SEQ:TOK], kcT[hp, 0:nc_keys], start=True, stop=True,
                           skip_group_check=True)
                        last = mm(bank(sb_, DEC, DEC, nc_keys), qT[hp, SEQ:TOK], kT[hp, SEQ:TOK],
                                  start=(nc_keys == 512), stop=True, skip_group_check=True)
                    last.then_inc(s_ready, 1)

                def turn_p(t):
                    m, h = BAND[t]
                    if t >= 1:
                        pe.wait_ge(pt_out, base + t)
                    wait_for(p_normed, base + t + 1, m == TT)
                    s = s_buf[t % 3]
                    if m < TT:
                        for c in range(keys_of(m) // P):
                            last = nc.tensor.transpose(bank(0, P, P, P * c), s[:, P * c:P * c + P], ident[:, :])
                    else:
                        for c in range(nc_keys // P):
                            nc.tensor.transpose(bank(0, DEC, P, DEC * c), s[0:DEC, P * c:P * c + P], ident[0:DEC, 0:DEC])
                        c = nc_keys // P
                        last = nc.tensor.transpose(bank(0, DEC, DEC, DEC * c), s[0:DEC, nc_keys:nc_keys + DEC],
                                                   ident[0:DEC, 0:DEC])
                    last.then_inc(pt_done, 1)

                def values(t):
                    m, h = BAND[t]
                    hp = slice(DH * h, DH * h + DH)
                    pe.wait_ge(pt_out, base + t + 1)
                    if t in (0, 8, 16):
                        pe.wait_ge(mix_made, 3 * pair + t // 8 + 1)
                    pT = pT_buf[t % 2]
                    if m < TT:
                        nk = keys_of(m) // P
                        out = ps[hp, 512 * O_BANK + P * (m % 4):512 * O_BANK + P * (m % 4) + P]
                        for c in range(nk):
                            last = mm(out, v_nat[:, m + 1 - nk + c, hp], pT[:, P * c:P * c + P],
                                      start=(c == 0), stop=(c == nk - 1), skip_group_check=True)
                    else:
                        out = ps[hp, 512 * O_BANK:512 * O_BANK + DEC]
                        for c in range(nc_keys // P):
                            mm(out, vc[:, c, hp], pT[:, DEC * c:DEC * c + DEC], start=(c == 0), stop=False,
                               skip_group_check=True)
                        c = nc_keys // P
                        last = mm(out, v_nat[0:DEC, 8, hp], pT[0:DEC, DEC * c:DEC * c + DEC], start=False, stop=True,
                                  skip_group_check=True)
                    last.then_inc(o_done if t in ENDS_B else bpv_done, 1)

                pe.wait_ge(proj_out, 3 * T + 9)
                for t in range(NSTEP_B + 3):
                    if t < NSTEP_B:
                        scores(t)
                    if 0 <= t - 2 < NSTEP_B:
                        turn_p(t - 2)
                    if 0 <= t - 3:
                        values(t - 3)

            def key_values(kind, T, kvn):
                project(T)
                project(T + 1)
                pe.wait_ge(proj_out, 3 * T + 6)
                turn_rows(kT, kvn, 0)
                turn_cache(kvn, 1 if kind == "b" else 4)
                project(T + 2)
                pe.wait_ge(proj_out, 3 * (T + 1) + 6)
                turn_rows(oT, kvn, 4)
                project(T + 3)

            with pe.Fori(0, NA) as i:
                T, pair, kvn = numbers("a", i)
                key_values("a", T, kvn)
                stick_breaking(i, T, pair, kvn)
            with pe.Fori(0, NB) as b:
                T, pair, kvn = numbers("b", b)
                key_values("b", T, kvn)
                for r in range(REP):
                    if r:
                        project(T + 2 + 2 * r)
                        project(T + 3 + 2 * r)
                    band(REP * b + r, 2, T + 2 + 2 * r, pair + r, kvn)
            with pe.Fori(0, NC) as c:
                T, pair, kvn = numbers("c", c)
                key_values("c", T, kvn)
                band(REP * NB + c, 5, T + 2, pair, kvn)

            pe.wait_ge(mix_made, 3 * PAIRS + 1)

            def out_chunk(g, n, first):
                toks = TOKSETS[g]
                for k in range(KT):
                    if first:
                        pe.wait_ge(mx_lo, k + 1)
                    pe.wait_ge(lo_made, P3 + KT * (NCH * g + n) + k + 1)
                    for j, tt in enumerate(toks):
                        if k == 0 and not first:
                            before = (0, NCH * len(TOKSETS[0]))[g] + len(toks) * n + j - len(toks) + 1
                            if g == 1 and isinstance(n, int) and n == 0:
                                before = NCH * len(TOKSETS[0])
                            pe.wait_ge(y_out, before)
                        th = act_hi_t[:, TOK * k + P * tt:TOK * k + P * tt + P]
                        tl = act_lo_t[:, TOK * k + P * tt:TOK * k + P * tt + P]
                        mm(bank(j), th, w_hi[:, k % RING, :], start=(k == 0), stop=False)
                        mm(bank(j), th, w_lo[:, k % RING, :], start=False, stop=False)
                        last = mm(bank(j), tl, w_hi[:, k % RING, :], start=False, stop=(k == KT - 1))
                        if k == KT - 1:
                            last.then_inc(y_done, 1)
                    if k < KT - 1:
                        last.then_inc(piece_used, 1)

            for g in (0, 1):
                out_chunk(g, 0, g == 0)
                with pe.Fori(1, NCH) as n:
                    out_chunk(g, n, False)

        @block.scalar
        def _(act):
            fn = nc.scalar.activation

            def x_std_of(t, s, rows, cs):
                act.wait_ge(x_in[s], cs)
                fn(ps[0:rows, 512 * X:512 * X + D], x_t[s][0:rows, :], ACT.Square,
                   accum_out=ssq[0:rows, s:s + 1]).then_inc(x_sq, 1)
                act.wait_ge(x_var, t + 1)
                fn(std_x[0:rows, s:s + 1], var[0:rows, s:s + 1], ACT.Sqrt).then_inc(x_std, 1)

            def x_high(t, rows):
                for g in range(4):
                    act.wait_ge(xt_done, 4 * t + g + 1)
                    b = (0, 1, 2, 7)[g]
                    fn(act_hi[:, 4 * g:4 * g + 4, bass.ds(P * t, rows)],
                       bank(b, 4 * rows).rearrange("p (k t) -> p k t", k=4), ACT.Copy).then_inc(x_hi, 1)

            x_std_of(0, 0, P, 16)
            with act.Fori(0, TT // 2 - 1) as i:
                x_std_of(2 * i + 1, 1, P, 16 * i + 16)
                x_high(2 * i, P)
                x_std_of(2 * i + 2, 0, P, 16 * i + 32)
                x_high(2 * i + 1, P)
            x_std_of(TT - 1, 1, P, 16 * (TT // 2))
            x_high(TT - 2, P)
            x_std_of(TT, 0, DEC, 16 * (TT // 2) + 16)
            x_high(TT - 1, P)
            x_high(TT, DEC)
            for q in range(4):
                act.wait_ge(raw_in[q], 16)
                fn(w_hi[:, q, :], w_raw[:, q, :], ACT.Copy).then_inc(hi_made, 1)

            def split(T, raw):
                for q in range(4):
                    act.wait_ge(raw_in[q], raw)
                    if q < 3:
                        act.wait_ge(piece_used, 3 * T + q + 1)
                    else:
                        act.wait_ge(proj_done, 3 * T + 3)
                    fn(w_hi[:, q, :], w_raw[:, q, :], ACT.Copy).then_inc(hi_made, 1)

            def rows_out(dst, kvn, lot):
                for g in range(3):
                    act.wait_ge(tr_done, TR * kvn + lot + g + 1)
                    if g < 2:
                        fn(dst[:, 4 * g:4 * g + 4, :], bank(X + g).rearrange("p (b c) -> p b c", b=4),
                           ACT.Copy).then_inc(tr_out, 1)
                    else:
                        fn(dst[0:DEC, 8, :], bank(X + g, P, DEC), ACT.Copy).then_inc(tr_out, 1)

            def keys_out(kind, kvn):
                act.wait_ge(k_stored, 32 * kvn + 1)
                rows_out(k_nat, kvn, 0)
                nb = 1 if kind == "b" else 4
                act.wait_ge(tr_done, TR * kvn + 4)
                fn(kcT[:, 0:P * nb], bank(X + 3, P * nb), ACT.Copy).then_inc(tr_out, 1)

            def values_out(kvn):
                act.wait_ge(v_stored, 32 * kvn + 1)
                rows_out(v_nat, kvn, 4)

            def gate(T, pair, kvn, st):
                act.wait_ge(proj_out, 3 * T + 6)
                act.wait_ge(tr_done, TR * kvn + TR)
                act.wait_ge(mix_stored, st)
                fn(oT[:, :], gT[:, :], ACT.Exp, scale=-1.0).then_inc(gate_exp, 1)

            def values_done(s, ends, steps, n, pair, t):
                if t in ends:
                    act.wait_ge(o_done, 3 * pair + ends.index(t) + 1)
                else:
                    act.wait_ge(s, (steps - 3) * n + sum(x not in ends for x in range(t + 1)))

            def stick_breaking(i, pair, kvn):
                act.wait_ge(k_stored, 32 * kvn + 33)
                base = NSTEP_A * i

                def span(t):
                    return (A_STEPS[t][3], BQ) if t < len(A_STEPS) else (0, 5 * DEC)

                for t in range(NSTEP_A + 2):
                    if t < NSTEP_A:
                        a, b = span(t)
                        act.wait_ge(z_ready, base + t + 1)
                        if t >= 2:
                            act.wait_ge(sp_ready, base + t - 1)
                        fn(e_buf[t % 2][:, a:b], bank(X + t % 4, b - a, P, a), ACT.Exp).then_inc(e_ready, 1)
                    u = t - 1
                    if 0 <= u < NSTEP_A:
                        a, b = span(u)
                        act.wait_ge(e_capped, base + u + 1)
                        fn(e_buf[u % 2][:, a:b], e_buf[u % 2][:, a:b], ACT.Ln, bias=1.0).then_inc(l_ready, 1)
                    u = t - 2
                    if u >= 0:
                        a, b = span(u)
                        act.wait_ge(t_done, base + u + 1)
                        if u >= 2:
                            values_done(pv_done, ENDS_A, NSTEP_A, i, pair, u - 2)
                        fn(wt_buf[u % 2][:, a:b], bank(X + u % 4, b - a, P, a), ACT.Exp).then_inc(w_ready, 1)

            def band(n, nb, pair):
                base = NSTEP_B * n
                ncb = 1 if nb == 2 else 4

                for t in range(NSTEP_B + 2):
                    if t < NSTEP_B:
                        m, h = BAND[t]
                        rows = P if m < TT else DEC
                        nk = P * min(m + 1, nb) if m < TT else P * ncb + DEC
                        act.wait_ge(s_biased, base + t + 1)
                        s = s_buf[t % 3][0:rows, 0:nk + (nb == 2)]
                        fn(s, s, ACT.Exp, bias=neg_max[0:rows, t:t + 1], scale=-1.0,
                           accum_out=row_sum[0:rows, t:t + 1]).then_inc(p_exp, 1)
                    u = t - 2
                    if u >= 0:
                        m, h = BAND[u]
                        act.wait_ge(pt_done, base + u + 1)
                        if u >= 2:
                            values_done(bpv_done, ENDS_B, NSTEP_B, n, pair, u - 2)
                        if m < TT:
                            nk = P * min(m + 1, nb)
                            fn(pT_buf[u % 2][:, 0:nk], bank(0, nk), ACT.Copy).then_inc(pt_out, 1)
                        else:
                            c = DEC * ncb
                            fn(pT_buf[u % 2][:, 0:c], bank(0, c), ACT.Copy)
                            fn(pT_buf[u % 2][0:DEC, c:c + DEC], bank(0, DEC, DEC, c), ACT.Copy).then_inc(pt_out, 1)

            act.preload_act_table_set("natural_log_exp_and_others")
            with act.Fori(0, NA) as i:
                T, pair, kvn = numbers("a", i)
                split(T, 16 * T + 32)
                split(T + 1, 16 * T + 48)
                keys_out("a", kvn)
                split(T + 2, 16 * T + 64)
                values_out(kvn)
                split(T + 3, 16 * T + 80)
                gate(T + 3, pair, kvn, stored("a", i))
                stick_breaking(i, pair, kvn)
            RB = 16 * 4 * NA
            UB = 16 * 2 + 32 * 2 * REP
            with act.Fori(0, NB) as b:
                T, pair, kvn = numbers("b", b)
                raw = RB + UB * b + 16
                split(T, raw + 16)
                split(T + 1, raw + 48)
                keys_out("b", kvn)
                split(T + 2, raw + 80)
                values_out(kvn)
                split(T + 3, raw + 112)
                for r in range(REP):
                    if r:
                        split(T + 2 + 2 * r, raw + 16 + 32 * (2 * r + 2))
                        split(T + 3 + 2 * r, raw + 16 + 32 * (2 * r + 2) + (32 if r < REP - 1 else 16))
                    gate(T + 3 + 2 * r, pair + r, kvn, stored("b", b, r))
                    if r == 0:
                        act.wait_ge(k_stored, 32 * kvn + 33)
                    band(REP * b + r, 2, pair + r)
            RC = RB + UB * NB
            with act.Fori(0, NC) as c:
                T, pair, kvn = numbers("c", c)
                raw = RC + 64 * c + 16
                split(T, raw + 16)
                split(T + 1, raw + 32)
                keys_out("c", kvn)
                split(T + 2, raw + 48)
                values_out(kvn)
                split(T + 3, raw + 64)
                gate(T + 3, pair, kvn, stored("c", c))
                act.wait_ge(k_stored, 32 * kvn + 33)
                band(REP * NB + c, 5, pair)
            R3 = RC + 64 * NC

            def mixed_hi(k):
                act.wait_ge(mixed_in[k // 4], 16 if k < KT - 1 else 32)
                fn(act_hi[:, k, :], act_lo[:, k, :].bitcast(F32), ACT.Copy).then_inc(mx_hi, 1)

            for k in range(4):
                mixed_hi(k)

            def out_chunk(g, n, last_chunk):
                toks = TOKSETS[g]
                pc = P3 + KT * (NCH * g + n)
                for k in range(KT - 4 if last_chunk else KT):
                    act.wait_ge(raw_in[k % RING], R3 + 16 * (4 * (NCH * g + n) + k // 4) + 32)
                    if k < KT - 1:
                        act.wait_ge(piece_used, 3 * TILES + (KT - 1) * (NCH * g + n) + k + 1)
                    else:
                        act.wait_ge(y_done, (0, NCH * len(TOKSETS[0]))[g] + len(toks) * (n + 1))
                    fn(w_hi[:, k % RING, :], w_raw[:, k % RING, :], ACT.Copy).then_inc(hi_made, 1)
                    if g == n == 0 and k + 4 < KT:
                        mixed_hi(k + 4)
                done = (0, NCH * len(TOKSETS[0]))[g]
                for j, tt in enumerate(toks):
                    rows = P if tt < TT else DEC
                    act.wait_ge(y_done, done + len(toks) * n + j + 1)
                    fn(y[0:rows, j, PIECE * n:PIECE * n + PIECE], bank(j, 512, rows), ACT.Square,
                       accum_out=ssq_y[0:rows, 4 * tt + n:4 * tt + n + 1]).then_inc(y_sq, 1)

            for g in (0, 1):
                for n in range(NCH):
                    if g == 1 and n == 0:
                        act.wait_ge(y_stored, 16 * len(TOKSETS[0]))
                    out_chunk(g, n, g == 1 and n == NCH - 1)
                for tt in TOKSETS[g]:
                    rows = P if tt < TT else DEC
                    act.wait_ge(yv_var, tt + 1)
                    fn(std_y[0:rows, tt:tt + 1], var_y[0:rows, tt:tt + 1], ACT.Sqrt).then_inc(yv_std, 1)

        @block.vector
        def _(dve):
            v = nc.vector
            for g in range(GROUPS):
                v.memset(small[:, 150 + g:151 + g], 0.0).then_inc(proj_out, 1)
            v.memset(small[:, 155:156], 0.0).then_inc(mix_made, 1)
            v.memset(kT[:, TOK:TOK + P - DEC], 0.0)
            v.memset(act_hi_t[:, KT * TOK:].bitcast(F32), 0.0)
            v.memset(act_lo_t[:, KT * TOK:].bitcast(F32), 0.0)
            dve.wait_ge(rel_in, 16)
            v.tensor_copy(ext[:, 0:P], tab[:, 2 * CLIP:2 * CLIP + 1].broadcast_to([H_C, P])).then_inc(ext_made, 1)
            v.tensor_copy(ext[:, P:P + 2 * CLIP], tab[:, 2 * CLIP - 1::-1]).then_inc(ext_made, 1)

            dve.wait_ge(gain_in, 16)

            def refined_rstd(r, var_, s, n):
                t = newton[0:r.shape[0], :]
                v.reciprocal(r, r).then_inc(s, 1)
                dve.wait_ge(s, 4 * n + 1)
                v.scalar_tensor_tensor(t, r, var_, r, ALU.mult, ALU.mult).then_inc(s, 1)
                dve.wait_ge(s, 4 * n + 2)
                v.tensor_scalar(t, t, -0.5, 1.5, ALU.mult, ALU.add).then_inc(s, 1)
                dve.wait_ge(s, 4 * n + 3)
                v.tensor_tensor(r, r, t, ALU.mult).then_inc(s, 1)
                dve.wait_ge(s, 4 * n + 4)

            def x_scale(t, s, rows):
                dve.wait_ge(x_sq, t + 1)
                v.tensor_scalar(var[0:rows, s:s + 1], ssq[0:rows, s:s + 1], 1.0 / D, EPS, ALU.mult, ALU.add).then_inc(x_var, 1)
                dve.wait_ge(x_std, t + 1)
                refined_rstd(std_x[0:rows, s:s + 1], var[0:rows, s:s + 1], x_rstd, t)
                v.scalar_tensor_tensor(x_t[s][0:rows, :], x_t[s][0:rows, :], std_x[0:rows, s:s + 1], pre_gain[0:rows, :],
                                       ALU.mult, ALU.mult).then_inc(x_norm, 1)

            def x_low(t, rows):
                for g in range(4):
                    dve.wait_ge(x_hi, 4 * t + g + 1)
                    b = (0, 1, 2, 7)[g]
                    v.tensor_tensor(act_lo[:, 4 * g:4 * g + 4, bass.ds(P * t, rows)],
                                    bank(b, 4 * rows).rearrange("p (k t) -> p k t", k=4),
                                    act_hi[:, 4 * g:4 * g + 4, bass.ds(P * t, rows)].bitcast(F32),
                                    ALU.subtract).then_inc(x_lo, 1)

            x_scale(0, 0, P)
            with dve.Fori(0, TT // 2 - 1) as i:
                x_scale(2 * i + 1, 1, P)
                x_low(2 * i, P)
                x_scale(2 * i + 2, 0, P)
                x_low(2 * i + 1, P)
            x_scale(TT - 1, 1, P)
            x_low(TT - 2, P)
            x_scale(TT, 0, DEC)
            x_low(TT - 1, P)
            x_low(TT, DEC)

            def low(pc, q):
                dve.wait_ge(hi_made, pc + 1)
                v.tensor_tensor(w_lo[:, q, :], w_raw[:, q, :], w_hi[:, q, :].bitcast(F32), ALU.subtract).then_inc(lo_made, 1)

            for q in range(4):
                low(q, q)

            def tile(T, dst, scale=None):
                for q in range(4):
                    if q == 3:
                        for g in range(GROUPS):
                            dve.wait_ge(proj_done, 3 * T + g + 1)
                            d = dst[:, GN * g:GN * g + GN]
                            if scale is None:
                                v.tensor_copy(d, bank(g, GN)).then_inc(proj_out, 1)
                            else:
                                v.tensor_scalar(d, bank(g, GN), scale, None, ALU.mult).then_inc(proj_out, 1)
                    low(4 * T + 4 + q, q)

            def make_gate(pair, c):
                part = slice(TOK // GATE_PARTS * c, TOK // GATE_PARTS * (c + 1))
                made = 3 * GATE_PARTS * pair + 3 * c
                dve.wait_ge(gate_exp, pair + 1)
                v.tensor_scalar(oT[:, part], oT[:, part], 1.0, None, ALU.add).then_inc(gate_made, 1)
                dve.wait_ge(gate_made, made + 1)
                v.reciprocal(oT[:, part], oT[:, part]).then_inc(gate_made, 1)
                dve.wait_ge(gate_made, made + 2)
                v.tensor_tensor(gT[:, part], gT[:, part], oT[:, part], ALU.mult).then_inc(gate_made, 1)

            def mix(pair, n):
                a, b = (0, BQ, SEQ)[n], (BQ, SEQ, TOK)[n]
                dve.wait_ge(o_done, 3 * pair + n + 1)
                dve.wait_ge(gate_made, 3 * GATE_PARTS * pair + 3 * -(-b * GATE_PARTS // TOK))
                v.tensor_tensor(oT[:, a:b], bank(O_BANK, b - a), gT[:, a:b], ALU.mult).then_inc(mix_made, 1)

            def stick_breaking(i, pair):
                base = NSTEP_A * i

                def span(t):
                    return (A_STEPS[t][3], BQ) if t < len(A_STEPS) else (0, 5 * DEC)

                for t in range(NSTEP_A + 1):
                    if t == 11:
                        mix(pair, 0)
                    if t < NSTEP_A:
                        a, b = span(t)
                        dve.wait_ge(e_ready, base + t + 1)
                        v.tensor_scalar(e_buf[t % 2][:, a:b], e_buf[t % 2][:, a:b], E_CAP, None, ALU.min).then_inc(e_capped, 1)
                    if 0 <= t - 2 < GATE_PARTS:
                        make_gate(pair, t - 2)
                    u = t - 1
                    if u >= 0:
                        a, b = span(u)
                        dve.wait_ge(l_ready, base + u + 1)
                        if u >= 2:
                            dve.wait_ge(t_done, base + u - 1)
                            dve.wait_ge(r_ready, R_BEFORE[-1] * i + R_BEFORE[min(u - 1, len(A_STEPS))])
                        v.tensor_tensor(sp_buf[u % 2][:, a:b], bank(X + u % 4, b - a, P, a), e_buf[u % 2][:, a:b],
                                        ALU.max).then_inc(sp_ready, 1)
                mix(pair, 1)
                mix(pair, 2)

            def band(n, nb, pair):
                base = NSTEP_B * n
                ncb = 1 if nb == 2 else 4
                for t in range(NSTEP_B + 1):
                    if t == 11:
                        mix(pair, 0)
                    if t < NSTEP_B:
                        m, h = BAND[t]
                        rows = P if m < TT else DEC
                        nk = P * min(m + 1, nb) if m < TT else P * ncb + DEC
                        a = P * nb - nk if m < TT else 0
                        if t == 0:
                            dve.wait_ge(bias_made, n + 1)
                        if t >= 3:
                            dve.wait_ge(pt_done, base + t - 2)
                        wait_apart(dve, s_ready, base + t + 1)
                        if nb == 2:
                            v.tensor_copy(s_buf[t % 3][0:rows, nk:nk + 1], neg_sink[0:rows, h:h + 1])
                        v.tensor_tensor_reduce(out=s_buf[t % 3][0:rows, 0:nk], in0=bank(X + 2 * (t % 2), nk, rows),
                                               in1=bias[0:rows, h, a:a + nk], scale=-1.0,
                                               scalar=neg_sink[0:rows, h:h + 1] if nb == 2 else -NEG,
                                               op0=ALU.add, op1=ALU.min, accum_out=neg_max[0:rows, t:t + 1]).then_inc(s_biased, 1)
                    if 0 <= t - 2 < GATE_PARTS:
                        make_gate(pair, t - 2)
                    u = t - 1
                    if u >= 0:
                        m, h = BAND[u]
                        rows = P if m < TT else DEC
                        nk = P * min(m + 1, nb) if m < TT else P * ncb + DEC
                        dve.wait_ge(p_exp, base + u + 1)
                        r = rden[0:rows, u:u + 1]
                        v.reciprocal(r, row_sum[0:rows, u:u + 1]).then_inc(den_made, 1)
                        dve.wait_ge(den_made, base + u + 1)
                        s = s_buf[u % 3][0:rows, 0:nk]
                        v.tensor_scalar(s, s, r, None, ALU.mult).then_inc(p_normed, 1)
                mix(pair, 1)
                mix(pair, 2)

            with dve.Fori(0, NA) as i:
                T, pair, kvn = numbers("a", i)
                tile(T, kT)
                dve.wait_ge(mix_stored, stored("a", i))
                tile(T + 1, oT)
                tile(T + 2, qT, SCALE)
                tile(T + 3, gT)
                stick_breaking(i, pair)
            with dve.Fori(0, NB) as b:
                T, pair, kvn = numbers("b", b)
                tile(T, kT)
                dve.wait_ge(mix_stored, stored("b", b))
                tile(T + 1, oT)
                for r in range(REP):
                    tile(T + 2 + 2 * r, qT, SCALE)
                    tile(T + 3 + 2 * r, gT)
                    dve.wait_ge(bias_in, 64 * (REP * b + r + 1))
                    v.tensor_scalar(neg_sink[:, :], sink_in[:, :], -1.0, None, ALU.mult).then_inc(bias_made, 1)
                    if r == 0:
                        dve.wait_ge(k_stored, 32 * kvn + 33)
                    band(REP * b + r, 2, pair + r)
            with dve.Fori(0, NC) as c:
                T, pair, kvn = numbers("c", c)
                tile(T, kT)
                dve.wait_ge(mix_stored, stored("c", c))
                tile(T + 1, oT)
                tile(T + 2, qT, SCALE)
                tile(T + 3, gT)
                dve.wait_ge(bias_in, 64 * REP * NB + 32 * c + 32)
                for h in (0, 1):
                    v.tensor_scalar(bias[:, h, 0:3 * P], mask_c[:, 0:3 * P], bias[:, h, 3 * P:3 * P + 1], None, ALU.add)
                    last = v.tensor_tensor(bias[:, h, 4 * P:5 * P], bias[:, h, 4 * P:5 * P], mask_c[:, 4 * P:5 * P], ALU.add)
                last.then_inc(bias_made, 1)
                dve.wait_ge(k_stored, 32 * kvn + 33)
                band(REP * NB + c, 5, pair)

            def mixed_lo(k):
                dve.wait_ge(mx_hi, k + 1)
                v.tensor_tensor(act_lo[:, k, :], act_lo[:, k, :].bitcast(F32), act_hi[:, k, :].bitcast(F32),
                                ALU.subtract).then_inc(mx_lo, 1)

            for k in range(4):
                mixed_lo(k)

            e = 0
            for g in (0, 1):
                toks = TOKSETS[g]
                done = (0, NCH * len(TOKSETS[0]))[g]
                for n in range(NCH):
                    pc = P3 + KT * (NCH * g + n)
                    for k in range(KT - 4 if g == 1 and n == NCH - 1 else KT):
                        low(pc + 4 + k, k % RING)
                        if g == n == 0 and k + 4 < KT:
                            mixed_lo(k + 4)
                    dve.wait_ge(post_in[n % 2], 16 * (2 * g + n // 2 + 1))
                    for j, tt in enumerate(toks):
                        rows = P if tt < TT else DEC
                        dve.wait_ge(y_sq, done + len(toks) * n + j + 1)
                        v.tensor_tensor(y[0:rows, j, PIECE * n:PIECE * n + PIECE], bank(j, 512, rows),
                                        post_gain[n % 2][0:rows, :], ALU.mult).then_inc(y_out, 1)
                for tt in toks:
                    rows = P if tt < TT else DEC
                    vy = var_y[0:rows, tt:tt + 1]
                    v.tensor_reduce(vy, ssq_y[0:rows, 4 * tt:4 * tt + 4], AX.X, ALU.add).then_inc(yv_sum, 1)
                    dve.wait_ge(yv_sum, tt + 1)
                    v.tensor_scalar(vy, vy, 1.0 / D, EPS, ALU.mult, ALU.add).then_inc(yv_var, 1)
                for j, tt in enumerate(toks):
                    rows = P if tt < TT else DEC
                    vy = var_y[0:rows, tt:tt + 1]
                    dve.wait_ge(yv_std, tt + 1)
                    sy = std_y[0:rows, tt:tt + 1]
                    refined_rstd(sy, vy, yv_rstd, tt)
                    dve.wait_ge(y_out, done + NCH * len(toks))
                    for half in (0, 1):
                        c = slice(1024 * half, 1024 * half + 1024)
                        dve.wait_ge(res_in[half], 16 * (e // 2 + 1))
                        v.scalar_tensor_tensor(y[0:rows, j, c], y[0:rows, j, c], sy, x_res[g][half][0:rows, :],
                                               ALU.mult, ALU.add).then_inc(fin_made, 1)
                        e += 1

        @block.gpsimd
        def _(pool):
            gp = nc.gpsimd
            gp.dma_start(tab, rel_bias[0]).then_inc(rel_in, 16)
            gp.memset(ident[:, :], 0.0).then_inc(consts, 1)
            gp.memset(ident_b[:, :], 0.0).then_inc(consts, 1)
            gp.memset(neg_tri[:, :], -1.0).then_inc(consts, 1)
            gp.memset(mask_b[:, :], NEG).then_inc(consts, 1)
            gp.memset(neg_ones[:, :], -1.0).then_inc(consts, 1)
            pool.wait_ge(consts, 5)
            for m in (ident, ident_b):
                gp.affine_select(out=m[:, :], in_=m[:, :], compare_op=ALU.not_equal, fill=1.0, base=0,
                                 pattern=[[-1, P]], channel_multiplier=1).then_inc(consts, 1)
            gp.affine_select(out=neg_tri[:, :], in_=neg_tri[:, :], compare_op=ALU.is_ge, fill=0.0, base=0,
                             pattern=[[-1, P]], channel_multiplier=1).then_inc(consts, 1)
            gp.affine_select(out=mask_b[:, :], in_=mask_b[:, :], compare_op=ALU.is_ge, fill=0.0, base=0,
                             pattern=[[-1, P]], channel_multiplier=1).then_inc(consts, 1)
            gp.memset(small[:, 156:157], 0.0).then_inc(k_stored, 1)
            gp.memset(small[:, 157:158], 0.0).then_inc(v_stored, 1)
            gp.memset(small[:, 158:159], 0.0).then_inc(mix_stored, 1)
            gp.memset(mask_c[:, :], 0.0).then_inc(consts, 1)
            pool.wait_ge(consts, CONSTS + 1)
            gp.memset(mask_c[0:64, 9 * CHUNK:10 * CHUNK], NEG).then_inc(consts, 1)
            pool.wait_ge(consts, CONSTS + 2)
            gp.memset(mask_c[64:128, 0:CHUNK], NEG).then_inc(consts, 1)
            pool.wait_ge(consts, CONSTS + 3)

            for cache, out, n in ((cache_b_k, bk_s, WINDOW), (cache_b_v, bv_s, WINDOW), (cache_c_k, ck_s, PAST), (cache_c_v, cv_s, PAST)):
                gp.dma_start(out[0, 0, 0:n - DEC].rearrange("t h d -> t (h d)"),
                             cache[0, 0, DEC:n].rearrange("t h d -> t (h d)")).then_inc(cache_moved, 16)

            def suffix_sums(i):
                base = NSTEP_A * i
                for t, (j, h, kt, c0, pos) in enumerate(A_STEPS):
                    if LAST[t]:
                        continue
                    if t:
                        pool.wait_ge(t_done, base + t)
                    if pos:
                        pool.wait_ge(r_ready, R_BEFORE[-1] * i + R_BEFORE[t])
                    wait_apart(pool, sp_ready, base + t + 1)
                    dst, s = r_buf[(pos + 1) % 2], sp_buf[t % 2]
                    if pos == 0:
                        gp.tensor_copy(dst[:, c0:BQ], s[:, c0:BQ]).then_inc(r_ready, 1)
                        continue
                    c1 = A_STEPS[t - 1][3]
                    if c0 < c1:
                        gp.tensor_copy(dst[:, c0:c1], s[:, c0:c1])
                    gp.tensor_tensor(dst[:, c1:BQ], r_buf[pos % 2][:, c1:BQ], s[:, c1:BQ], ALU.add).then_inc(r_ready, 1)

            with pool.Fori(0, NA) as i:
                suffix_sums(i)
            for tt in range(TT + 1):
                pool.wait_ge(fin_made, 2 * tt + 2)
                j = tt if tt < 4 else tt - 4
                if tt < TT:
                    gp.dma_start(y_prompt[0, P * tt:P * tt + P, :], y[:, j, :]).then_inc(y_stored, 16)
                else:
                    gp.dma_start(y_sample[0], y[0:DEC, j, :]).then_inc(y_stored, 16)
            pool.wait_ge(y_stored, 16 * (TT + 1))
            pool.wait_ge(k_stored, 32 * (NA + NB + NC) + 1)
            pool.wait_ge(v_stored, 32 * (NA + NB + NC) + 1)
            pool.wait_ge(cache_moved, 64)


def alibi_table():
    def geometric(m):
        start = 2.0 ** (-8.0 / m)
        return [start ** (i + 1) for i in range(m)]
    c = 2 ** int(np.floor(np.log2(H_B)))
    slopes = np.asarray(geometric(c) + geometric(2 * c)[0::2][:H_B - c], np.float32)
    q, k = np.arange(P)[:, None], np.arange(2 * P)[None] - P
    dc = q // CHUNK - k // CHUNK
    seen = (dc >= 0) & (dc <= WINDOW // CHUNK)
    dist = np.abs(q - k).astype(np.float32)
    return np.where(seen[None], -slopes[:, None, None] * dist[None], np.float32(NEG)).astype(np.float32)


_INS = ['x_prompt', 'x_sample', 'cache_a_k', 'cache_a_v', 'cache_b_k', 'cache_b_v', 'cache_c_k', 'cache_c_v',
        'norm_pre', 'norm_post', 'w_in', 'w_out', 'attn_sinks', 'rel_bias']
_OUTS = [(1, SEQ, D), (1, DEC, D), (1, 1, SEQ, H_A, DH), (1, 1, SEQ, H_A, DH), (1, 1, DEC, H_A, DH), (1, 1, DEC, H_A, DH),
         (1, 1, WINDOW, H_BKV, DH), (1, 1, WINDOW, H_BKV, DH), (1, 1, WINDOW, H_BKV, DH), (1, 1, WINDOW, H_BKV, DH),
         (1, 1, PAST, H_C, DH), (1, 1, PAST, H_C, DH), (1, 1, PAST, H_C, DH), (1, 1, PAST, H_C, DH)]


def kernel(**inputs):
    import concourse.bacc as _bacc
    from concourse.bass_utils import run_bass_kernel_spmd as _run

    nc = _bacc.Bacc("TRN2", target_bir_lowering=False, num_devices=1)
    arrays, args = {}, []
    for name in _INS + ['alibi']:
        a = alibi_table() if name == 'alibi' else np.ascontiguousarray(inputs[name])
        arrays[f"in_{name}_dram"] = a
        args.append(nc.dram_tensor(f"in_{name}_dram", a.shape, mybir.dt.from_np(a.dtype), kind="ExternalInput").ap())
    for i, shape in enumerate(_OUTS):
        args.append(nc.dram_tensor(f"out_{i}_dram", shape, F32, kind="ExternalOutput").ap())
    build(nc, *args)
    r = _run(nc, [arrays], core_ids=[0])
    return tuple(r.results[0][f"out_{i}_dram"] for i in range(len(_OUTS)))
```

```python
from contextlib import ExitStack

import concourse.bass as bass
import numpy as np
from concourse import mybir

F32, F32R, BF16 = mybir.dt.float32, mybir.dt.float32r, mybir.dt.bfloat16
ALU, ACT, AX = mybir.AluOpType, mybir.ActivationFunctionType, mybir.AxisListType

P = 128
D = 2048
KT = D // P
SEQ, DEC, PAST = 1024, 32, 512
TOK = SEQ + DEC
GROUPS = 3
GN = TOK // GROUPS
DH = 64
CHUNK = 64
H_A, H_B, H_BKV, H_C = 12, 12, 4, 8
W_A, W_B, KV_B, W_C = H_A * DH, H_B * DH, H_BKV * DH, H_C * DH
NA, NB, NC = H_A // 2, H_BKV // 2, H_C // 2
REP = H_B // H_BKV
WINDOW, CLIP = 128, 128
EPS = 1e-6
SCALE = DH ** -0.5
NEG = -1e30
E_CAP = 2.0 ** 60

A_Q, A_K, A_V, A_G = 0, W_A, 2 * W_A, 3 * W_A
B_Q = 4 * W_A
B_K, B_V, B_G = B_Q + W_B, B_Q + W_B + KV_B, B_Q + W_B + 2 * KV_B
C_Q = B_G + W_B
C_K, C_V, C_G = C_Q + W_C, C_Q + 2 * W_C, C_Q + 3 * W_C

PIECE = 512
RING = 4
TILES = 4 * NA + (2 + 2 * REP) * NB + 4 * NC
PAIRS = NA + REP * NB + NC
TT = SEQ // P
TR = 7
GATE_PARTS = 8
BQ = 4 * P


def a_steps():
    steps = []
    for j in range(SEQ // BQ):
        for h in range(2):
            for pos, i in enumerate(range(4 * j + 3, -1, -1)):
                steps.append((j, h, i, max(0, P * (i - 4 * j)), pos))
    return steps


A_STEPS = a_steps()
NSTEP_A = len(A_STEPS) + 2
LAST = [i == 0 for _, _, i, _, _ in A_STEPS]
R_BEFORE = [sum(not x for x in LAST[:t]) for t in range(len(LAST) + 1)]
BAND = [(m, h) for m in range(TT + 1) for h in range(2)]
NSTEP_B = len(BAND)
ENDS_A, ENDS_B = (7, 23, 25), (7, 15, 17)


def build(nc, x_prompt, x_sample, cache_a_k, cache_a_v, cache_b_k, cache_b_v, cache_c_k, cache_c_v,
          norm_pre, norm_post, w_in, w_out, attn_sinks, rel_bias, alibi,
          y_prompt, y_sample, ak_p, av_p, ak_s, av_s, bk_p, bv_p, bk_s, bv_s, ck_p, cv_p, ck_s, cv_s):
    ctx = ExitStack()
    with ctx:
        def sb(name, shape, dt=F32):
            return ctx.enter_context(nc.sbuf_tensor(name, shape, dt))

        def sem(name):
            return ctx.enter_context(nc.semaphore(name))

        act_hi_t = sb("act_hi", [P, KT * TOK + P - DEC], F32R)
        act_lo_t = sb("act_lo", [P, KT * TOK + P - DEC], F32R)
        act_hi = act_hi_t[:, 0:KT * TOK].rearrange("p (k t) -> p k t", k=KT)
        act_lo = act_lo_t[:, 0:KT * TOK].rearrange("p (k t) -> p k t", k=KT)
        w_raw = sb("w_raw", [P, RING, PIECE])
        w_hi = sb("w_hi", [P, RING, PIECE], F32R)
        w_lo = sb("w_lo", [P, RING, PIECE], F32R)
        arena = sb("arena", [P, 11616])
        at = [0]

        def cut(n):
            at[0] += n
            return arena[:, at[0] - n:at[0]]

        kT = cut(TOK + P - DEC)
        qT, gT, oT = cut(TOK), cut(TOK), cut(TOK)
        v_nat = cut(9 * P).rearrange("p (b c) -> p b c", b=9)
        kc = cut(4 * P).rearrange("p (b c) -> p b c", b=4)
        vc = cut(4 * P).rearrange("p (b c) -> p b c", b=4)
        kcT = cut(4 * P)
        work0 = at[0]
        work = cut(4608)
        k_nat = work[:, 0:9 * P].rearrange("p (b c) -> p b c", b=9)
        e_buf = [work[:, 512 * i:512 * i + 512] for i in (0, 1)]
        sp_buf = [work[:, 512 * i:512 * i + 512] for i in (2, 3, 8)]
        r_buf = [work[:, 512 * i:512 * i + 512] for i in (4, 5)]
        wt_buf = [work[:, 512 * i:512 * i + 512] for i in (6, 7)]
        s_buf = [work[:, 640 * i:640 * i + 640] for i in (0, 1, 2)]
        pT_buf = [work[:, 640 * i:640 * i + 640] for i in (3, 4)]
        bias = work[:, 3200:4480].rearrange("p (h c) -> p h c", h=2)
        x_t = [arena[:, 1152 + D * i:1152 + D * i + D] for i in range(3)]
        pre_gain = arena[:, 1152 + 3 * D:1152 + 4 * D]
        squares_x = arena[:, 1152 + 4 * D:1152 + 4 * D + D // 2].bitcast(BF16)
        y = arena[:, 0:5 * D].rearrange("p (t c) -> p t c", t=5)
        post_gain = [arena[:, 5 * D + 512 * i:5 * D + 512 * i + 512] for i in (0, 1)]
        x_res = [[arena[:, 4 * D + 1024 * i:4 * D + 1024 * i + 1024] for i in (0, 1)],
                 [w_raw[:, 2 * i:2 * i + 2, :].rearrange("p a b -> p (a b)") for i in (0, 1)]]

        mask_c = sb("mask_c", [P, 640])
        ident = sb("ident", [P, P])
        neg_tri = sb("neg_tri", [P, P])
        neg_ones = sb("neg_ones", [P, P])
        ident_b = sb("ident_b", [P, P], BF16)
        mask_b = sb("mask_b", [P, P], BF16)
        small = sb("small", [P, 170])
        ssq, var = small[:, 0:9], small[:, 9:18]
        neg_max, row_sum, rden = (small[:, 20 + 18 * i:38 + 18 * i] for i in range(3))
        sink_in, neg_sink = small[:, 92:94], small[:, 94:96]
        ssq_y = small[:, 96:132]
        std_x, std_y, newton = small[:, 141:144], small[:, 160:169], small[:, 144:145]
        var_y = small[:, 132:141]
        tab = arena[0:H_C, 10400:10400 + 2 * CLIP + 1]
        ext = arena[0:H_C, 10400 + 2 * P + 8:10400 + 2 * P + 8 + 384]

        ps = ctx.enter_context(nc.psum_tensor("ps", [P, 8 * 512], F32))

        def bank(b, n=512, r=P, c=0):
            return ps[0:r, 512 * b + c:512 * b + c + n]

        X = 3
        O_BANK = 7
        Z_BANKS = (3, 4, 5, 6, 0, 1)

        mixed_d = nc.dram_tensor("mixed_scratch", (D, TOK), F32, kind="Internal").ap()
        ext_d = nc.dram_tensor("rel_ext", (H_C, 384), F32, kind="Internal")
        toep_d = nc.dram_tensor("rel_toeplitz", (H_C, P, 2 * P), F32, kind="Internal").ap()

        x_in = [sem(f"x_in{i}") for i in range(3)]
        gain_in = sem("gain_in")
        x_sq, x_var, x_std, x_rstd, x_norm = (sem(n) for n in ("x_sq", "x_var", "x_std", "x_rstd", "x_norm"))
        xt_done, x_hi, x_lo = sem("xt_done"), sem("x_hi"), sem("x_lo")
        consts = sem("consts")
        rel_in, ext_made, ext_out, toep_out = sem("rel_in"), sem("ext_made"), sem("ext_out"), sem("toep_out")
        raw_in = [sem(f"raw_in{i}") for i in range(RING)]
        hi_made, lo_made, piece_used = sem("hi_made"), sem("lo_made"), sem("piece_used")
        proj_done, proj_out = sem("proj_done"), sem("proj_out")
        tr_done, tr_out = sem("tr_done"), sem("tr_out")
        kc_in, vc_in = sem("kc_in"), sem("vc_in")
        k_stored, v_stored, cache_moved = sem("k_stored"), sem("v_stored"), sem("cache_moved")
        z_ready, e_ready, e_capped, l_ready = sem("z_ready"), sem("e_ready"), sem("e_capped"), sem("l_ready")
        sp_ready, r_ready, t_done, w_ready, pv_done = (sem(n) for n in ("sp_ready", "r_ready", "t_done", "w_ready", "pv_done"))
        gate_exp, gate_made = sem("gate_exp"), sem("gate_made")
        o_done, mix_made, mix_stored = sem("o_done"), sem("mix_made"), sem("mix_stored")
        bias_in, bias_made = sem("bias_in"), sem("bias_made")
        s_ready, s_biased, p_exp, den_made, p_normed = (sem(n) for n in ("s_ready", "s_biased", "p_exp", "den_made", "p_normed"))
        pt_done, pt_out, bpv_done = sem("pt_done"), sem("pt_out"), sem("bpv_done")
        mixed_in = [sem(f"mixed_in{i}") for i in range(4)]
        mx_hi, mx_lo = sem("mx_hi"), sem("mx_lo")
        post_in = [sem("post_in0"), sem("post_in1")]
        y_done, y_sq, y_out = sem("y_done"), sem("y_sq"), sem("y_out")
        yv_sum, yv_var, yv_std, yv_rstd = (sem(n) for n in ("yv_sum", "yv_var", "yv_std", "yv_rstd"))
        res_in = [sem("res_in0"), sem("res_in1")]
        fin_made, y_stored = sem("fin_made"), sem("y_stored")

        w_in_v = w_in[0].rearrange("(k p) c -> p k c", p=P)
        w_out_v = w_out[0].rearrange("(k p) c -> p k c", p=P)
        CONSTS = 9

        passed = {e.engine: sem(f"passed_{n}") for n, e in (("pe", nc.tensor), ("dve", nc.vector), ("pool", nc.gpsimd))}

        def a_tile(i, n):
            return 4 * i + n

        def b_tile(b, n):
            return 4 * NA + (2 + 2 * REP) * b + n

        def c_tile(c, n):
            return 4 * NA + (2 + 2 * REP) * NB + 4 * c + n

        def stored(kind, i, r=0):
            if kind == "a":
                return 16 * i + 1
            if kind == "b":
                return 16 * NA + 32 * (REP * i + r) + 1
            return 16 * NA + 32 * REP * NB + 16 * i + 1

        MIX_ALL = 16 * NA + 32 * REP * NB + 16 * NC + 1

        PARTS = (("a", NA), ("b", NB), ("c", NC))

        def numbers(kind, i):
            if kind == "a":
                return 4 * i, i, i
            if kind == "b":
                return b_tile(i, 0), NA + REP * i, NA + i
            return c_tile(i, 0), NA + REP * NB + i, NA + NB + i

        TOKSETS = ((0, 1, 2, 3), (4, 5, 6, 7, 8))
        NCH = D // PIECE
        END_PIECES, LAST_PIECES = 2, 4
        P3 = 4 * TILES

        def out_count(chunks):
            return sum(len(TOKSETS[c // NCH]) for c in range(chunks))

        def score_bank(nb, t):
            return (X + t % 4, 4) if nb == 2 else (X + 2 * (t % 2), 2)

        def turned(nb, t, n, r=P, c=0):
            return bank(t % 2 if nb == 2 else 0, n, r, c)

        block = ctx.enter_context(nc.Block())

        def wait_apart(eng, s, value):
            eng.wait_ge(s, value)
            eng.sem_inc(passed[eng.engine], 1)

        @block.sync
        def _(sp):
            def cols(T, base, halves=None):
                for q in range(4):
                    if not (isinstance(T, int) and T == 0):
                        sp.wait_ge(lo_made, 4 * T + q - 3)
                    dst = w_raw[:, q, :].rearrange("p (k c) -> p k c", k=4)
                    if halves is None:
                        sp.dma_start(dst, w_in_v[:, 4 * q:4 * q + 4, bass.ds(base, P)]).then_inc(raw_in[q], 16)
                    else:
                        for s, b in enumerate(halves):
                            sp.dma_start(dst[:, :, 64 * s:64 * s + 64],
                                         w_in_v[:, 4 * q:4 * q + 4, bass.ds(b, 64)]).then_inc(raw_in[q], 8 * 2)

            def caches(kind, i):
                _, pair, kv = numbers(kind, i)
                if not isinstance(i, int) or kind != "a" or i > 0:
                    sp.wait_ge(o_done, 3 * pair)
                nb = 1 if kind == "b" else 4
                ck, cv = {"a": (cache_a_k, cache_a_v), "b": (cache_b_k, cache_b_v), "c": (cache_c_k, cache_c_v)}[kind]
                for cache, dst, s in ((ck, kc, kc_in), (cv, vc, vc_in)):
                    src = cache[0, 0].rearrange("(b p) h d -> p b (h d)", p=P)
                    sp.dma_start(dst[:, 0:nb, :], src[:, :, bass.ds(P * i, P)]).then_inc(s, 16)

            def store(kind, i, which):
                kvn = numbers(kind, i)[2]
                prompt, sample = {"a": ((ak_p, ak_s), (av_p, av_s)), "b": ((bk_p, bk_s), (bv_p, bv_s)),
                                  "c": ((ck_p, ck_s), (cv_p, cv_s))}[kind][which]
                src, s = ((k_nat, k_stored), (v_nat, v_stored))[which]
                keep = {"a": SEQ, "b": WINDOW, "c": PAST}[kind]
                total = {"a": DEC, "b": WINDOW, "c": PAST}[kind]
                sp.wait_ge(tr_out, TR * kvn + (3, TR)[which])
                sp.dma_start(prompt[0, 0].rearrange("(b p) h d -> p b (h d)", p=P)[:, :, bass.ds(P * i, P)],
                             src[:, (SEQ - keep) // P:8, :]).then_inc(s, 16)
                sp.dma_start(sample[0, 0].rearrange("t h d -> t (h d)")[total - DEC:total, bass.ds(P * i, P)],
                             src[0:DEC, 8, :]).then_inc(s, 16)

            def store_mixed(pair, rows):
                sp.wait_ge(mix_made, 3 * pair + 4)
                n = P // len(rows)
                for s, row in enumerate(rows):
                    sp.dma_start(mixed_d[bass.ds(row, n), :], oT[n * s:n * s + n, :]).then_inc(mix_stored, 16)

            def unit_a(i, nxt):
                caches("a", i)
                cols(a_tile(i, 1), A_V + P * i)
                cols(a_tile(i, 2), A_Q + P * i)
                cols(a_tile(i, 3), A_G + P * i)
                store("a", i, 0)
                nxt()
                store("a", i, 1)
                store_mixed(i, [P * i])

            for t in range(TT + 1):
                if t >= 3:
                    sp.wait_ge(xt_done, 4 * (t - 3) + 4)
                if t < TT:
                    sp.dma_start(x_t[t % 3], x_prompt[0, P * t:P * t + P, :]).then_inc(x_in[t % 3], 16)
                else:
                    sp.dma_start(x_t[t % 3][0:DEC, :], x_sample[0]).then_inc(x_in[t % 3], 16)
                if t == 0:
                    sp.dma_start(pre_gain, norm_pre[0].partition_broadcast(P)).then_inc(gain_in, 16)
                if t == 2:
                    cols(0, A_K)
            sp.wait_ge(ext_made, 2)
            sp.dma_start(ext_d.ap(), ext).then_inc(ext_out, 16)
            sp.wait_ge(ext_out, 16)
            sp.dma_start(toep_d, bass.AP(ext_d, P - 1, [[384, H_C], [-1, P], [1, 2 * P]])).then_inc(toep_out, 16)
            sp.wait_ge(x_lo, 4 * (TT + 1))

            unit_a(0, lambda: cols(a_tile(1, 0), A_K + P))
            with sp.Fori(1, NA - 1) as i:
                unit_a(i, lambda: cols(a_tile(i + 1, 0), A_K + P * i + P))
            unit_a(NA - 1, lambda: cols(b_tile(0, 0), B_K))

            for b in range(NB):
                caches("b", b)
                cols(b_tile(b, 1), B_V + P * b)
                for r in range(REP):
                    h0 = 2 * REP * b + r
                    pair = NA + REP * b + r
                    cols(b_tile(b, 2 + 2 * r), None, [B_Q + DH * h0, B_Q + DH * (h0 + REP)])
                    if r == 1:
                        store("b", b, 1)
                    if r:
                        store_mixed(pair - 1, [W_A + DH * (h0 - 1), W_A + DH * (h0 - 1 + REP)])
                    sp.wait_ge(o_done, 3 * pair)
                    for s in (0, 1):
                        sp.dma_start(bias[:, s, 0:2 * P], alibi[h0 + REP * s]).then_inc(bias_in, 16)
                        sp.dma_start(sink_in[:, s:s + 1],
                                     attn_sinks[0, h0 + REP * s:h0 + REP * s + 1].partition_broadcast(P)).then_inc(bias_in, 16)
                    cols(b_tile(b, 3 + 2 * r), None, [B_G + DH * h0, B_G + DH * (h0 + REP)])
                    if r == 0:
                        store("b", b, 0)
                if b + 1 < NB:
                    cols(b_tile(b + 1, 0), B_K + P * (b + 1))
                else:
                    cols(c_tile(0, 0), C_K)
                store_mixed(pair, [W_A + DH * h0, W_A + DH * (h0 + REP)])

            def unit_c(c, nxt):
                caches("c", c)
                cols(c_tile(c, 1), C_V + P * c)
                cols(c_tile(c, 2), C_Q + P * c)
                for s in (0, 1):
                    sp.dma_start(bias[:, s, 3 * P:5 * P], toep_d[bass.ds(2 * c + s, 1)].rearrange("o q k -> (o q) k")).then_inc(bias_in, 16)
                cols(c_tile(c, 3), C_G + P * c)
                store("c", c, 0)
                if nxt:
                    cols(c_tile(c + 1, 0), C_K + P * c + P)
                else:
                    for k in range(RING):
                        out_piece(0, 0, k)
                store("c", c, 1)
                if not nxt:
                    sp.wait_ge(proj_done, 3 * TILES)
                    sp.wait_ge(mix_stored, MIX_ALL - 16)
                    for j in range(4):
                        mixed_load(4 * j, min(4 * j + 4, KT - 1), mixed_in[j])
                store_mixed(NA + REP * NB + c, [W_A + W_B + P * c])

            def out_piece(g, n, k):
                pc = P3 + KT * NCH * g + KT * n + k
                sp.wait_ge(lo_made, pc - 3)
                sp.dma_start(w_raw[:, k % RING, :], w_out_v[:, k, bass.ds(PIECE * n, PIECE)]).then_inc(raw_in[k % RING], 16)

            def mixed_load(k0, k1, s):
                sp.dma_start(act_lo[:, k0:k1, :].bitcast(F32),
                             mixed_d[P * k0:P * k1, :].rearrange("(k p) t -> p k t", p=P)).then_inc(s, 16)

            sp.wait_ge(toep_out, 16)
            with sp.Fori(0, NC - 1) as c:
                unit_c(c, True)
            unit_c(NC - 1, False)

            sp.wait_ge(mix_stored, MIX_ALL)
            mixed_load(KT - 1, KT, mixed_in[3])

            def gain_chunk(g, n):
                if not (g == 0 and n < 2):
                    sp.wait_ge(y_out, out_count(NCH * g + n - 1))
                sp.dma_start(post_gain[n % 2], norm_post[0, PIECE * n:PIECE * n + PIECE].partition_broadcast(P)).then_inc(post_in[n % 2], 16)

            def residual(g, e):
                if e >= 2:
                    sp.wait_ge(fin_made, e - 1)
                tt, half = divmod(e, 2)
                c = slice(1024 * half, 1024 * half + 1024)
                if tt < TT:
                    sp.dma_start(x_res[g][half], x_prompt[0, P * tt:P * tt + P, c]).then_inc(res_in[half], 16)
                else:
                    sp.dma_start(x_res[g][half][0:DEC, :], x_sample[0, :, c]).then_inc(res_in[half], 16)

            halves = 2 * len(TOKSETS[0])
            for g in range(2):
                for n in range(NCH):
                    gain_chunk(g, n)
                    for k in range(RING, KT):
                        out_piece(g, n, k)
                        if g == 1 and n == 0 and 2 <= k - 6 < halves:
                            residual(0, k - 6)
                    if n + 1 < NCH:
                        for k in range(RING):
                            out_piece(g, n + 1, k)
                    elif g == 0:
                        for k in range(RING):
                            out_piece(1, 0, k)
                        residual(0, 0)
                        residual(0, 1)
            sp.wait_ge(lo_made, P3 + 2 * KT * NCH)
            for e in range(halves, 2 * (TT + 1)):
                residual(1, e)

        @block.tensor
        def _(pe):
            mm = nc.tensor.matmul

            def wait_for(s, value, apart):
                if apart:
                    wait_apart(pe, s, value)
                else:
                    pe.wait_ge(s, value)

            def x_tile(t):
                rows = P if t < TT else DEC
                for g in range(4):
                    pe.wait_ge(x_norm, t + 1)
                    if t:
                        pe.wait_ge(x_lo, 4 * t + g - 3)
                    for c in range(4):
                        last = nc.tensor.transpose(bank(X + g, rows, P, rows * c),
                                                   x_t[t % 3][0:rows, P * (4 * g + c):P * (4 * g + c) + P],
                                                   ident[0:rows, 0:rows])
                    last.then_inc(xt_done, 1)

            def product(g, q):
                for kk in range(4):
                    k = 4 * q + kk
                    wh, wl = w_hi[:, q, P * kk:P * kk + P], w_lo[:, q, P * kk:P * kk + P]
                    ah, al = act_hi[:, k, GN * g:GN * g + GN], act_lo[:, k, GN * g:GN * g + GN]
                    mm(bank(g, GN), wh, ah, start=(k == 0), stop=False)
                    mm(bank(g, GN), wh, al, start=False, stop=False)
                    last = mm(bank(g, GN), wl, ah, start=False, stop=(k == KT - 1))
                return last

            def project(T):
                for q in range(4):
                    pe.wait_ge(lo_made, 4 * T + q + 1)
                    for g in range(GROUPS):
                        if q == 0:
                            pe.wait_ge(proj_out, 3 * T + g + 1)
                        last = product(g, q)
                        if q == 3:
                            last.then_inc(proj_done, 1)
                    if q < 3:
                        last.then_inc(piece_used, 1)

            def first_project(g):
                pe.wait_ge(x_lo, 4 * (3 * g + 3))
                pe.wait_ge(proj_out, g + 1)
                for q in range(4):
                    pe.wait_ge(lo_made, q + 1)
                    last = product(g, q)
                    if q == 3:
                        last.then_inc(proj_done, 1)
                    elif g == GROUPS - 1:
                        last.then_inc(piece_used, 1)

            pe.wait_ge(consts, CONSTS)
            for t in range(TT + 1):
                x_tile(t)
                if t in (3, 6):
                    first_project(t // 3 - 1)
            first_project(GROUPS - 1)

            def turn_rows(src, kvn, lot):
                for g in range(3):
                    b = X + g
                    if lot == 4:
                        pe.wait_ge(tr_out, TR * kvn + g + 1)
                    if g < 2:
                        for n in range(4):
                            t = 4 * g + n
                            last = nc.tensor.transpose(bank(b, P, P, P * n), src[:, P * t:P * t + P], ident[:, :])
                    else:
                        last = nc.tensor.transpose(bank(b, P, DEC), src[:, SEQ:TOK], ident[:, :])
                    last.then_inc(tr_done, 1)

            def turn_cache(kvn, nb):
                pe.wait_ge(kc_in, 16 * (kvn + 1))
                for n in range(nb):
                    last = nc.tensor.transpose(bank(X + 3, P, P, P * n), kc[:, n, :], ident[:, :])
                last.then_inc(tr_done, 1)

            def stick_breaking(i, T, pair, kvn):
                pe.wait_ge(proj_out, 3 * (T + 2) + 6)
                pe.wait_ge(tr_out, TR * kvn + TR)
                base = NSTEP_A * i

                def scores(t):
                    zb = Z_BANKS[t % 6]
                    if t == Z_BANKS.index(0):
                        pe.wait_ge(proj_out, 3 * (T + 3) + 6)
                    if t >= 6:
                        pe.wait_ge(w_ready, base + t - 5)
                    if t < len(A_STEPS):
                        j, h, kt, c0, _ = A_STEPS[t]
                        hp = slice(DH * h, DH * h + DH)
                        last = mm(bank(zb, BQ - c0, P, c0), kT[hp, P * kt:P * kt + P], qT[hp, BQ * j + c0:BQ * j + BQ],
                                  start=True, stop=False, skip_group_check=True)
                        if kt >= 4 * j:
                            last = mm(bank(zb, P, P, c0), ident_b[:, :], mask_b[:, :], start=False, stop=False,
                                      skip_group_check=True)
                    else:
                        h = t - len(A_STEPS)
                        hp = slice(DH * h, DH * h + DH)
                        for blk in range(5):
                            keys = kcT[hp, P * blk:P * blk + P] if blk < 4 else kT[hp, SEQ:SEQ + P]
                            mm(bank(zb, DEC, P, DEC * blk), keys, qT[hp, SEQ:TOK], start=(blk == 0), stop=False,
                               skip_group_check=True)
                        last = mm(bank(zb, DEC, P, DEC * 4), ident_b[:, :], mask_b[:, 0:DEC],
                                  start=False, stop=False, skip_group_check=True)
                    last.then_inc(z_ready, 1)

                def suffix(t):
                    zb = Z_BANKS[t % 6]
                    pe.wait_ge(sp_ready, base + t + 1)
                    sp_t = sp_buf[t % 3]
                    if t < len(A_STEPS):
                        j, h, kt, c0, pos = A_STEPS[t]
                        last = mm(bank(zb, BQ - c0, P, c0), neg_tri[:, :], sp_t[:, c0:BQ], start=False, stop=(pos == 0),
                                  skip_group_check=True)
                        if pos:
                            pe.wait_ge(r_ready, R_BEFORE[-1] * i + R_BEFORE[t])
                            c1 = A_STEPS[t - 1][3]
                            last = mm(bank(zb, BQ - c1, P, c1), neg_ones[:, :], r_buf[pos % 2][:, c1:BQ],
                                      start=False, stop=True, skip_group_check=True)
                    else:
                        mm(bank(zb, 5 * DEC), neg_tri[:, :], sp_t[:, 0:5 * DEC], start=False, stop=False,
                           skip_group_check=True)
                        for blk in range(1, 5):
                            later = sp_t[:, DEC * blk:DEC * blk + DEC].unsqueeze(1).broadcast_to([P, blk, DEC])
                            last = mm(bank(zb, DEC * blk), neg_ones[:, :], later, start=False, stop=(blk == 4),
                                      skip_group_check=True)
                    last.then_inc(t_done, 1)

                def values(t):
                    pe.wait_ge(w_ready, base + t + 1)
                    wt = wt_buf[t % 2]
                    if t in (0, 8, 24):
                        pe.wait_ge(mix_made, 3 * pair + (0, 8, 24).index(t) + 1)
                    if t < len(A_STEPS):
                        j, h, kt, c0, pos = A_STEPS[t]
                        hp = slice(DH * h, DH * h + DH)
                        last = mm(ps[hp, 512 * O_BANK + c0:512 * O_BANK + BQ], v_nat[:, kt, hp], wt[:, c0:BQ],
                                  start=(pos == 0), stop=(kt == 0), skip_group_check=True)
                    else:
                        h = t - len(A_STEPS)
                        hp = slice(DH * h, DH * h + DH)
                        for blk in range(5):
                            rows = P if blk < 4 else DEC
                            v = vc[:, blk, hp] if blk < 4 else v_nat[0:DEC, 8, hp]
                            last = mm(ps[hp, 512 * O_BANK:512 * O_BANK + DEC], v, wt[0:rows, DEC * blk:DEC * blk + DEC],
                                      start=(blk == 0), stop=(blk == 4), skip_group_check=True)
                    last.then_inc(o_done if t in ENDS_A else pv_done, 1)

                pe.wait_ge(vc_in, 16 * (kvn + 1))
                for t in range(NSTEP_A + 4):
                    if t < NSTEP_A:
                        scores(t)
                    if 0 <= t - 3 < NSTEP_A:
                        suffix(t - 3)
                    if 0 <= t - 4:
                        values(t - 4)

            def band(n, nb, T, pair, kvn):
                pe.wait_ge(tr_out, TR * kvn + TR)
                pe.wait_ge(vc_in, 16 * (kvn + 1))
                pe.wait_ge(proj_out, 3 * (T + 1) + 6)
                base = NSTEP_B * n
                nc_keys = P if nb == 2 else 4 * P

                def keys_of(m):
                    return P * min(m + 1, nb)

                def scores(t):
                    m, h = BAND[t]
                    hp = slice(DH * h, DH * h + DH)
                    sb_, before = score_bank(nb, t)
                    if t >= before:
                        wait_for(s_biased, base + t - before + 1, m == TT)
                    if m < TT:
                        nk = keys_of(m)
                        k0 = P * (m + 1) - nk
                        for c in range(0, nk, 512):
                            w = min(512, nk - c)
                            last = mm(bank(sb_, w, P, c), qT[hp, P * m:P * m + P], kT[hp, k0 + c:k0 + c + w],
                                      start=True, stop=True, skip_group_check=True)
                    else:
                        mm(bank(sb_, nc_keys, DEC), qT[hp, SEQ:TOK], kcT[hp, 0:nc_keys], start=True, stop=True,
                           skip_group_check=True)
                        last = mm(bank(sb_, DEC, DEC, nc_keys), qT[hp, SEQ:TOK], kT[hp, SEQ:TOK],
                                  start=(nc_keys == 512), stop=True, skip_group_check=True)
                    last.then_inc(s_ready, 1)

                def turn_p(t):
                    m, h = BAND[t]
                    before = 2 if nb == 2 else 1
                    if t >= before:
                        pe.wait_ge(pt_out, base + t - before + 1)
                    wait_for(p_normed, base + t + 1, m == TT)
                    s = s_buf[t % 3]
                    if m < TT:
                        for c in range(keys_of(m) // P):
                            last = nc.tensor.transpose(turned(nb, t, P, P, P * c), s[:, P * c:P * c + P], ident[:, :])
                    else:
                        for c in range(nc_keys // P):
                            nc.tensor.transpose(turned(nb, t, DEC, P, DEC * c), s[0:DEC, P * c:P * c + P], ident[0:DEC, 0:DEC])
                        c = nc_keys // P
                        last = nc.tensor.transpose(turned(nb, t, DEC, DEC, DEC * c), s[0:DEC, nc_keys:nc_keys + DEC],
                                                   ident[0:DEC, 0:DEC])
                    last.then_inc(pt_done, 1)

                def values(t):
                    m, h = BAND[t]
                    hp = slice(DH * h, DH * h + DH)
                    pe.wait_ge(pt_out, base + t + 1)
                    if t in (0, 8, 16):
                        pe.wait_ge(mix_made, 3 * pair + t // 8 + 1)
                    pT = pT_buf[t % 2]
                    if m < TT:
                        nk = keys_of(m) // P
                        out = ps[hp, 512 * O_BANK + P * (m % 4):512 * O_BANK + P * (m % 4) + P]
                        for c in range(nk):
                            last = mm(out, v_nat[:, m + 1 - nk + c, hp], pT[:, P * c:P * c + P],
                                      start=(c == 0), stop=(c == nk - 1), skip_group_check=True)
                    else:
                        out = ps[hp, 512 * O_BANK:512 * O_BANK + DEC]
                        for c in range(nc_keys // P):
                            mm(out, vc[:, c, hp], pT[:, DEC * c:DEC * c + DEC], start=(c == 0), stop=False,
                               skip_group_check=True)
                        c = nc_keys // P
                        last = mm(out, v_nat[0:DEC, 8, hp], pT[0:DEC, DEC * c:DEC * c + DEC], start=False, stop=True,
                                  skip_group_check=True)
                    last.then_inc(o_done if t in ENDS_B else bpv_done, 1)

                for t in range(NSTEP_B + 3):
                    if t < NSTEP_B:
                        scores(t)
                    if 0 <= t - 2 < NSTEP_B:
                        turn_p(t - 2)
                    if 0 <= t - 3:
                        values(t - 3)

            def key_values(kind, T, kvn):
                project(T + 1)
                pe.wait_ge(proj_out, 3 * T + 6)
                turn_rows(kT, kvn, 0)
                turn_cache(kvn, 1 if kind == "b" else 4)
                project(T + 2)
                pe.wait_ge(proj_out, 3 * (T + 1) + 6)
                turn_rows(oT, kvn, 4)
                project(T + 3)

            with pe.Fori(0, NA) as i:
                T, pair, kvn = numbers("a", i)
                key_values("a", T, kvn)
                stick_breaking(i, T, pair, kvn)
                project(T + 4)
            with pe.Fori(0, NB) as b:
                T, pair, kvn = numbers("b", b)
                key_values("b", T, kvn)
                for r in range(REP):
                    if r:
                        project(T + 2 + 2 * r)
                        project(T + 3 + 2 * r)
                    band(REP * b + r, 2, T + 2 + 2 * r, pair + r, kvn)
                project(T + 2 + 2 * REP)

            def unit_c(c):
                T, pair, kvn = numbers("c", c)
                key_values("c", T, kvn)
                band(REP * NB + c, 5, T + 2, pair, kvn)

            with pe.Fori(0, NC - 1) as c:
                unit_c(c)
                project(c_tile(c, 4))
            unit_c(NC - 1)

            pe.wait_ge(mix_made, 3 * PAIRS + 1)

            def out_chunk(g, n, first, last_chunk=False):
                toks = TOKSETS[g]
                ends = LAST_PIECES if last_chunk else END_PIECES
                by_piece = [(k, j) for k in range(KT - ends) for j in range(len(toks))]
                by_tile = [(k, j) for j in range(len(toks)) for k in range(KT - ends, KT)]
                for k, j in by_piece + by_tile:
                    if j == 0:
                        if first:
                            pe.wait_ge(mx_lo, k + 1)
                        pe.wait_ge(lo_made, P3 + KT * (NCH * g + n) + k + 1)
                    if k == 0 and not first:
                        before = (0, NCH * len(TOKSETS[0]))[g] + len(toks) * n + j - len(toks) + 1
                        if g == 1 and isinstance(n, int) and n == 0:
                            before = min(j + 1, len(TOKSETS[0])) + (NCH - 1) * len(TOKSETS[0])
                        pe.wait_ge(y_out, before)
                    th = act_hi_t[:, TOK * k + P * toks[j]:TOK * k + P * toks[j] + P]
                    tl = act_lo_t[:, TOK * k + P * toks[j]:TOK * k + P * toks[j] + P]
                    mm(bank(j), th, w_hi[:, k % RING, :], start=(k == 0), stop=False)
                    mm(bank(j), th, w_lo[:, k % RING, :], start=False, stop=False)
                    last = mm(bank(j), tl, w_hi[:, k % RING, :], start=False, stop=(k == KT - 1))
                    if k == KT - 1:
                        last.then_inc(y_done, 1)
                    elif j == len(toks) - 1:
                        last.then_inc(piece_used, 1)

            out_chunk(0, 0, True)
            with pe.Fori(1, NCH) as n:
                out_chunk(0, n, False)
            out_chunk(1, 0, False)
            with pe.Fori(1, NCH - 1) as n:
                out_chunk(1, n, False)
            out_chunk(1, NCH - 1, False, True)

        @block.scalar
        def _(act):
            fn = nc.scalar.activation

            def x_std_of(t):
                rows = P if t < TT else DEC
                act.wait_ge(x_in[t % 3], 16 * (t // 3 + 1))
                fn(squares_x[0:rows, :], x_t[t % 3][0:rows, :], ACT.Square, accum_out=ssq[0:rows, t:t + 1]).then_inc(x_sq, 1)
                act.wait_ge(x_var, t + 1)
                fn(std_x[0:rows, t % 3:t % 3 + 1], var[0:rows, t:t + 1], ACT.Sqrt).then_inc(x_std, 1)

            def x_high(t):
                rows = P if t < TT else DEC
                for g in range(4):
                    act.wait_ge(xt_done, 4 * t + g + 1)
                    fn(act_hi[:, 4 * g:4 * g + 4, P * t:P * t + rows],
                       bank(X + g, 4 * rows).rearrange("p (k t) -> p k t", k=4), ACT.Copy).then_inc(x_hi, 1)

            x_std_of(0)
            for t in range(TT + 1):
                if t < TT:
                    x_std_of(t + 1)
                x_high(t)
                if t == 1:
                    for q in range(4):
                        act.wait_ge(raw_in[q], 16)
                        fn(w_hi[:, q, :], w_raw[:, q, :], ACT.Copy).then_inc(hi_made, 1)

            def split(T, raw):
                for q in range(4):
                    act.wait_ge(raw_in[q], raw)
                    if q < 3:
                        act.wait_ge(piece_used, 3 * T + q + 1)
                    else:
                        act.wait_ge(proj_done, 3 * T + 3)
                    fn(w_hi[:, q, :], w_raw[:, q, :], ACT.Copy).then_inc(hi_made, 1)

            def rows_out(dst, kvn, lot):
                for g in range(3):
                    act.wait_ge(tr_done, TR * kvn + lot + g + 1)
                    if g < 2:
                        fn(dst[:, 4 * g:4 * g + 4, :], bank(X + g).rearrange("p (b c) -> p b c", b=4),
                           ACT.Copy).then_inc(tr_out, 1)
                    else:
                        fn(dst[0:DEC, 8, :], bank(X + g, P, DEC), ACT.Copy).then_inc(tr_out, 1)

            def keys_out(kind, kvn):
                act.wait_ge(k_stored, 32 * kvn + 1)
                rows_out(k_nat, kvn, 0)
                nb = 1 if kind == "b" else 4
                act.wait_ge(tr_done, TR * kvn + 4)
                fn(kcT[:, 0:P * nb], bank(X + 3, P * nb), ACT.Copy).then_inc(tr_out, 1)

            def values_out(kvn):
                act.wait_ge(v_stored, 32 * kvn + 1)
                rows_out(v_nat, kvn, 4)

            def gate(T, pair, kvn, st):
                act.wait_ge(proj_out, 3 * T + 6)
                act.wait_ge(tr_done, TR * kvn + TR)
                act.wait_ge(mix_stored, st)
                fn(oT[:, :], gT[:, :], ACT.Exp, scale=-1.0).then_inc(gate_exp, 1)

            def values_done(s, ends, steps, n, pair, t):
                if t in ends:
                    act.wait_ge(o_done, 3 * pair + ends.index(t) + 1)
                else:
                    act.wait_ge(s, (steps - 3) * n + sum(x not in ends for x in range(t + 1)))

            def stick_breaking(i, pair, kvn):
                act.wait_ge(k_stored, 32 * kvn + 33)
                base = NSTEP_A * i

                def span(t):
                    return (A_STEPS[t][3], BQ) if t < len(A_STEPS) else (0, 5 * DEC)

                for t in range(NSTEP_A + 3):
                    if t < NSTEP_A:
                        a, b = span(t)
                        act.wait_ge(z_ready, base + t + 1)
                        if t >= 2:
                            act.wait_ge(sp_ready, base + t - 1)
                        fn(e_buf[t % 2][:, a:b], bank(Z_BANKS[t % 6], b - a, P, a), ACT.Exp).then_inc(e_ready, 1)
                    u = t - 1
                    if 0 <= u < NSTEP_A:
                        a, b = span(u)
                        act.wait_ge(e_capped, base + u + 1)
                        fn(e_buf[u % 2][:, a:b], e_buf[u % 2][:, a:b], ACT.Ln, bias=1.0).then_inc(l_ready, 1)
                    u = t - 3
                    if u >= 0:
                        a, b = span(u)
                        act.wait_ge(t_done, base + u + 1)
                        if u >= 2:
                            values_done(pv_done, ENDS_A, NSTEP_A, i, pair, u - 2)
                        fn(wt_buf[u % 2][:, a:b], bank(Z_BANKS[u % 6], b - a, P, a), ACT.Exp).then_inc(w_ready, 1)

            def band(n, nb, pair):
                base = NSTEP_B * n
                ncb = 1 if nb == 2 else 4

                for t in range(NSTEP_B + 2):
                    if t < NSTEP_B:
                        m, h = BAND[t]
                        rows = P if m < TT else DEC
                        nk = P * min(m + 1, nb) if m < TT else P * ncb + DEC
                        act.wait_ge(s_biased, base + t + 1)
                        s = s_buf[t % 3][0:rows, 0:nk + (nb == 2)]
                        fn(s, s, ACT.Exp, bias=neg_max[0:rows, t:t + 1], scale=-1.0,
                           accum_out=row_sum[0:rows, t:t + 1]).then_inc(p_exp, 1)
                    u = t - 2
                    if u >= 0:
                        m, h = BAND[u]
                        act.wait_ge(pt_done, base + u + 1)
                        if u >= 2:
                            values_done(bpv_done, ENDS_B, NSTEP_B, n, pair, u - 2)
                        if m < TT:
                            nk = P * min(m + 1, nb)
                            fn(pT_buf[u % 2][:, 0:nk], turned(nb, u, nk), ACT.Copy).then_inc(pt_out, 1)
                        else:
                            c = DEC * ncb
                            fn(pT_buf[u % 2][:, 0:c], turned(nb, u, c), ACT.Copy)
                            fn(pT_buf[u % 2][0:DEC, c:c + DEC], turned(nb, u, DEC, DEC, c), ACT.Copy).then_inc(pt_out, 1)

            act.preload_act_table_set("natural_log_exp_and_others")
            with act.Fori(0, NA) as i:
                T, pair, kvn = numbers("a", i)
                split(T, 16 * T + 32)
                split(T + 1, 16 * T + 48)
                keys_out("a", kvn)
                split(T + 2, 16 * T + 64)
                values_out(kvn)
                split(T + 3, 16 * T + 80)
                gate(T + 3, pair, kvn, stored("a", i))
                stick_breaking(i, pair, kvn)
            RB = 16 * 4 * NA
            UB = 16 * 2 + 32 * 2 * REP
            with act.Fori(0, NB) as b:
                T, pair, kvn = numbers("b", b)
                raw = RB + UB * b + 16
                split(T, raw + 16)
                split(T + 1, raw + 48)
                keys_out("b", kvn)
                split(T + 2, raw + 80)
                values_out(kvn)
                split(T + 3, raw + 112)
                for r in range(REP):
                    if r:
                        split(T + 2 + 2 * r, raw + 16 + 32 * (2 * r + 2))
                        split(T + 3 + 2 * r, raw + 16 + 32 * (2 * r + 2) + (32 if r < REP - 1 else 16))
                    gate(T + 3 + 2 * r, pair + r, kvn, stored("b", b, r))
                    if r == 0:
                        act.wait_ge(k_stored, 32 * kvn + 33)
                    band(REP * b + r, 2, pair + r)
            RC = RB + UB * NB
            with act.Fori(0, NC) as c:
                T, pair, kvn = numbers("c", c)
                raw = RC + 64 * c + 16
                split(T, raw + 16)
                split(T + 1, raw + 32)
                keys_out("c", kvn)
                split(T + 2, raw + 48)
                values_out(kvn)
                split(T + 3, raw + 64)
                gate(T + 3, pair, kvn, stored("c", c))
                act.wait_ge(k_stored, 32 * kvn + 33)
                band(REP * NB + c, 5, pair)
            R3 = RC + 64 * NC

            def mixed_hi(k):
                act.wait_ge(mixed_in[k // 4], 16 if k < KT - 1 else 32)
                fn(act_hi[:, k, :], act_lo[:, k, :].bitcast(F32), ACT.Copy).then_inc(mx_hi, 1)

            for k in range(4):
                mixed_hi(k)

            def std_of(tt):
                rows = P if tt < TT else DEC
                act.wait_ge(yv_var, tt + 1)
                fn(std_y[0:rows, tt:tt + 1], var_y[0:rows, tt:tt + 1], ACT.Sqrt).then_inc(yv_std, 1)

            def squares(g, n, j):
                rows = P if TOKSETS[g][j] < TT else DEC
                act.wait_ge(y_done, out_count(NCH * g + n) + j + 1)
                fn(y[0:rows, j, PIECE * n:PIECE * n + PIECE], bank(j, 512, rows), ACT.Square,
                   accum_out=ssq_y[0:rows, 4 * TOKSETS[g][j] + n:4 * TOKSETS[g][j] + n + 1]).then_inc(y_sq, 1)

            def next_hi(g, n, k):
                act.wait_ge(raw_in[k % RING], R3 + 16 * (4 * (NCH * g + n) + k // 4) + 32)
                if k < KT - 1:
                    act.wait_ge(piece_used, 3 * TILES + (KT - 1) * (NCH * g + n) + k + 1)
                else:
                    act.wait_ge(y_done, out_count(NCH * g + n + 1))
                fn(w_hi[:, k % RING, :], w_raw[:, k % RING, :], ACT.Copy).then_inc(hi_made, 1)

            for g in (0, 1):
                for n in range(NCH):
                    last_chunk = g == 1 and n == NCH - 1
                    tiles = len(TOKSETS[g])
                    for k in range(KT - (LAST_PIECES if last_chunk else END_PIECES)):
                        next_hi(g, n, k)
                        if g == n == 0 and k + 4 < KT:
                            mixed_hi(k + 4)
                        if g == 1 and n == k == 0:
                            for tt in TOKSETS[0]:
                                std_of(tt)
                    if g == 1 and n == 0:
                        act.wait_ge(y_stored, 16 * len(TOKSETS[0]))
                    if last_chunk:
                        for j in range(tiles):
                            squares(g, n, j)
                            if j:
                                std_of(TOKSETS[1][j - 1])
                        std_of(TOKSETS[1][-1])
                        continue
                    for j in range(tiles - 1):
                        squares(g, n, j)
                    for k in range(KT - END_PIECES, KT):
                        next_hi(g, n, k)
                    squares(g, n, tiles - 1)

        @block.vector
        def _(dve):
            v = nc.vector
            for g in range(GROUPS):
                v.memset(small[:, 150 + g:151 + g], 0.0).then_inc(proj_out, 1)
            v.memset(small[:, 155:156], 0.0).then_inc(mix_made, 1)
            v.memset(kT[:, TOK:TOK + P - DEC], 0.0)
            v.memset(act_hi_t[:, KT * TOK:].bitcast(F32), 0.0)
            v.memset(act_lo_t[:, KT * TOK:].bitcast(F32), 0.0)
            dve.wait_ge(rel_in, 16)
            v.tensor_copy(ext[:, 0:P], tab[:, 2 * CLIP:2 * CLIP + 1].broadcast_to([H_C, P])).then_inc(ext_made, 1)
            v.tensor_copy(ext[:, P:P + 2 * CLIP], tab[:, 2 * CLIP - 1::-1]).then_inc(ext_made, 1)

            dve.wait_ge(gain_in, 16)

            def refined_rstd(r, var_, s, n):
                t = newton[0:r.shape[0], :]
                v.reciprocal(r, r).then_inc(s, 1)
                dve.wait_ge(s, 4 * n + 1)
                v.scalar_tensor_tensor(t, r, var_, r, ALU.mult, ALU.mult).then_inc(s, 1)
                dve.wait_ge(s, 4 * n + 2)
                v.tensor_scalar(t, t, -0.5, 1.5, ALU.mult, ALU.add).then_inc(s, 1)
                dve.wait_ge(s, 4 * n + 3)
                v.tensor_tensor(r, r, t, ALU.mult).then_inc(s, 1)
                dve.wait_ge(s, 4 * n + 4)

            def x_scale(t):
                rows = P if t < TT else DEC
                r, var_ = std_x[0:rows, t % 3:t % 3 + 1], var[0:rows, t:t + 1]
                dve.wait_ge(x_sq, t + 1)
                v.tensor_scalar(var_, ssq[0:rows, t:t + 1], 1.0 / D, EPS, ALU.mult, ALU.add).then_inc(x_var, 1)
                dve.wait_ge(x_std, t + 1)
                refined_rstd(r, var_, x_rstd, t)
                v.scalar_tensor_tensor(x_t[t % 3][0:rows, :], x_t[t % 3][0:rows, :], r, pre_gain[0:rows, :],
                                       ALU.mult, ALU.mult).then_inc(x_norm, 1)

            def x_low(t):
                rows = P if t < TT else DEC
                for g in range(4):
                    dve.wait_ge(x_hi, 4 * t + g + 1)
                    v.tensor_tensor(act_lo[:, 4 * g:4 * g + 4, P * t:P * t + rows],
                                    bank(X + g, 4 * rows).rearrange("p (k t) -> p k t", k=4),
                                    act_hi[:, 4 * g:4 * g + 4, P * t:P * t + rows].bitcast(F32),
                                    ALU.subtract).then_inc(x_lo, 1)

            def low(pc, q):
                dve.wait_ge(hi_made, pc + 1)
                v.tensor_tensor(w_lo[:, q, :], w_raw[:, q, :], w_hi[:, q, :].bitcast(F32), ALU.subtract).then_inc(lo_made, 1)

            x_scale(0)
            for t in range(TT + 1):
                if t < TT:
                    x_scale(t + 1)
                x_low(t)
                if t == 1:
                    for q in range(4):
                        low(q, q)

            def tile(T, dst, scale=None):
                for q in range(4):
                    if q == 3:
                        for g in range(GROUPS):
                            dve.wait_ge(proj_done, 3 * T + g + 1)
                            d = dst[:, GN * g:GN * g + GN]
                            if scale is None:
                                v.tensor_copy(d, bank(g, GN)).then_inc(proj_out, 1)
                            else:
                                v.tensor_scalar(d, bank(g, GN), scale, None, ALU.mult).then_inc(proj_out, 1)
                    low(4 * T + 4 + q, q)

            def make_gate(pair, c):
                part = slice(TOK // GATE_PARTS * c, TOK // GATE_PARTS * (c + 1))
                made = 3 * GATE_PARTS * pair + 3 * c
                dve.wait_ge(gate_exp, pair + 1)
                v.tensor_scalar(oT[:, part], oT[:, part], 1.0, None, ALU.add).then_inc(gate_made, 1)
                dve.wait_ge(gate_made, made + 1)
                v.reciprocal(oT[:, part], oT[:, part]).then_inc(gate_made, 1)
                dve.wait_ge(gate_made, made + 2)
                v.tensor_tensor(gT[:, part], gT[:, part], oT[:, part], ALU.mult).then_inc(gate_made, 1)

            def mix(pair, n):
                a, b = (0, BQ, SEQ)[n], (BQ, SEQ, TOK)[n]
                dve.wait_ge(o_done, 3 * pair + n + 1)
                dve.wait_ge(gate_made, 3 * GATE_PARTS * pair + 3 * -(-b * GATE_PARTS // TOK))
                v.tensor_tensor(oT[:, a:b], bank(O_BANK, b - a), gT[:, a:b], ALU.mult).then_inc(mix_made, 1)

            def stick_breaking(i, pair):
                base = NSTEP_A * i

                def span(t):
                    return (A_STEPS[t][3], BQ) if t < len(A_STEPS) else (0, 5 * DEC)

                for t in range(NSTEP_A + 1):
                    if t == 12:
                        mix(pair, 0)
                    if t < NSTEP_A:
                        a, b = span(t)
                        dve.wait_ge(e_ready, base + t + 1)
                        v.tensor_scalar(e_buf[t % 2][:, a:b], e_buf[t % 2][:, a:b], E_CAP, None, ALU.min).then_inc(e_capped, 1)
                    if 0 <= t - 2 < GATE_PARTS:
                        make_gate(pair, t - 2)
                    u = t - 1
                    if u >= 0:
                        a, b = span(u)
                        dve.wait_ge(l_ready, base + u + 1)
                        if u >= 3:
                            dve.wait_ge(t_done, base + u - 2)
                            dve.wait_ge(r_ready, R_BEFORE[-1] * i + R_BEFORE[min(u - 2, len(A_STEPS))])
                        v.tensor_tensor(sp_buf[u % 3][:, a:b], bank(Z_BANKS[u % 6], b - a, P, a), e_buf[u % 2][:, a:b],
                                        ALU.max).then_inc(sp_ready, 1)
                mix(pair, 1)
                mix(pair, 2)

            def band(n, nb, pair):
                base = NSTEP_B * n
                ncb = 1 if nb == 2 else 4
                for t in range(NSTEP_B + 1):
                    if t == 11:
                        mix(pair, 0)
                    if t < NSTEP_B:
                        m, h = BAND[t]
                        rows = P if m < TT else DEC
                        nk = P * min(m + 1, nb) if m < TT else P * ncb + DEC
                        a = P * nb - nk if m < TT else 0
                        if t == 0:
                            dve.wait_ge(bias_made, n + 1)
                        if t >= 3:
                            dve.wait_ge(pt_done, base + t - 2)
                        wait_apart(dve, s_ready, base + t + 1)
                        if nb == 2:
                            v.tensor_copy(s_buf[t % 3][0:rows, nk:nk + 1], neg_sink[0:rows, h:h + 1])
                        v.tensor_tensor_reduce(out=s_buf[t % 3][0:rows, 0:nk], in0=bank(score_bank(nb, t)[0], nk, rows),
                                               in1=bias[0:rows, h, a:a + nk], scale=-1.0,
                                               scalar=neg_sink[0:rows, h:h + 1] if nb == 2 else -NEG,
                                               op0=ALU.add, op1=ALU.min, accum_out=neg_max[0:rows, t:t + 1]).then_inc(s_biased, 1)
                    if 0 <= t - 2 < GATE_PARTS:
                        make_gate(pair, t - 2)
                    u = t - 1
                    if u >= 0:
                        m, h = BAND[u]
                        rows = P if m < TT else DEC
                        nk = P * min(m + 1, nb) if m < TT else P * ncb + DEC
                        dve.wait_ge(p_exp, base + u + 1)
                        r = rden[0:rows, u:u + 1]
                        v.reciprocal(r, row_sum[0:rows, u:u + 1]).then_inc(den_made, 1)
                        dve.wait_ge(den_made, base + u + 1)
                        s = s_buf[u % 3][0:rows, 0:nk]
                        v.tensor_scalar(s, s, r, None, ALU.mult).then_inc(p_normed, 1)
                mix(pair, 1)
                mix(pair, 2)

            with dve.Fori(0, NA) as i:
                T, pair, kvn = numbers("a", i)
                tile(T, kT)
                dve.wait_ge(mix_stored, stored("a", i))
                tile(T + 1, oT)
                tile(T + 2, qT, SCALE)
                tile(T + 3, gT)
                stick_breaking(i, pair)
            with dve.Fori(0, NB) as b:
                T, pair, kvn = numbers("b", b)
                tile(T, kT)
                dve.wait_ge(mix_stored, stored("b", b))
                tile(T + 1, oT)
                for r in range(REP):
                    tile(T + 2 + 2 * r, qT, SCALE)
                    tile(T + 3 + 2 * r, gT)
                    dve.wait_ge(bias_in, 64 * (REP * b + r + 1))
                    v.tensor_scalar(neg_sink[:, :], sink_in[:, :], -1.0, None, ALU.mult).then_inc(bias_made, 1)
                    if r == 0:
                        dve.wait_ge(k_stored, 32 * kvn + 33)
                    band(REP * b + r, 2, pair + r)
            with dve.Fori(0, NC) as c:
                T, pair, kvn = numbers("c", c)
                tile(T, kT)
                dve.wait_ge(mix_stored, stored("c", c))
                tile(T + 1, oT)
                tile(T + 2, qT, SCALE)
                tile(T + 3, gT)
                dve.wait_ge(bias_in, 64 * REP * NB + 32 * c + 32)
                for h in (0, 1):
                    v.tensor_scalar(bias[:, h, 0:3 * P], mask_c[:, 0:3 * P], bias[:, h, 3 * P:3 * P + 1], None, ALU.add)
                    last = v.tensor_tensor(bias[:, h, 4 * P:5 * P], bias[:, h, 4 * P:5 * P], mask_c[:, 4 * P:5 * P], ALU.add)
                last.then_inc(bias_made, 1)
                dve.wait_ge(k_stored, 32 * kvn + 33)
                band(REP * NB + c, 5, pair)

            def mixed_lo(k):
                dve.wait_ge(mx_hi, k + 1)
                v.tensor_tensor(act_lo[:, k, :], act_lo[:, k, :].bitcast(F32), act_hi[:, k, :].bitcast(F32),
                                ALU.subtract).then_inc(mx_lo, 1)

            for k in range(4):
                mixed_lo(k)

            def rows_of(tt):
                return P if tt < TT else DEC

            def with_gain(g, n, j):
                rows = rows_of(TOKSETS[g][j])
                dve.wait_ge(post_in[n % 2], 16 * (2 * g + n // 2 + 1))
                dve.wait_ge(y_sq, out_count(NCH * g + n) + j + 1)
                v.tensor_tensor(y[0:rows, j, PIECE * n:PIECE * n + PIECE], bank(j, 512, rows),
                                post_gain[n % 2][0:rows, :], ALU.mult).then_inc(y_out, 1)

            def variance(tt):
                vy = var_y[0:rows_of(tt), tt:tt + 1]
                v.tensor_reduce(vy, ssq_y[0:rows_of(tt), 4 * tt:4 * tt + 4], AX.X, ALU.add).then_inc(yv_sum, 1)
                dve.wait_ge(yv_sum, tt + 1)
                v.tensor_scalar(vy, vy, 1.0 / D, EPS, ALU.mult, ALU.add).then_inc(yv_var, 1)

            def finish(g, j, half):
                tt = TOKSETS[g][j]
                rows = rows_of(tt)
                sy = std_y[0:rows, tt:tt + 1]
                if half == 0:
                    dve.wait_ge(yv_std, tt + 1)
                    refined_rstd(sy, var_y[0:rows, tt:tt + 1], yv_rstd, tt)
                c = slice(1024 * half, 1024 * half + 1024)
                dve.wait_ge(y_out, out_count(NCH * (g + 1) - 1) + j + 1)
                dve.wait_ge(res_in[half], 16 * (tt + 1))
                v.scalar_tensor_tensor(y[0:rows, j, c], y[0:rows, j, c], sy, x_res[g][half][0:rows, :],
                                       ALU.mult, ALU.add).then_inc(fin_made, 1)

            for g in (0, 1):
                tiles = len(TOKSETS[g])
                for n in range(NCH):
                    last_chunk = g == 1 and n == NCH - 1
                    following = P3 + KT * (NCH * g + n) + 4
                    for k in range(KT - (LAST_PIECES if last_chunk else END_PIECES)):
                        low(following + k, k % RING)
                        if g == n == 0 and k + 4 < KT:
                            mixed_lo(k + 4)
                        if g == 1 and n == 0 and k < 2 * len(TOKSETS[0]):
                            finish(0, k // 2, k % 2)
                    if last_chunk:
                        for j in range(tiles):
                            with_gain(g, n, j)
                            variance(TOKSETS[1][j])
                            if j:
                                finish(1, j - 1, 0)
                                finish(1, j - 1, 1)
                        finish(1, tiles - 1, 0)
                        finish(1, tiles - 1, 1)
                        continue
                    for j in range(tiles - 1):
                        with_gain(g, n, j)
                    for k in range(KT - END_PIECES, KT):
                        low(following + k, k % RING)
                    with_gain(g, n, tiles - 1)
                if g == 0:
                    for tt in TOKSETS[0]:
                        variance(tt)

        @block.gpsimd
        def _(pool):
            gp = nc.gpsimd
            gp.dma_start(tab, rel_bias[0]).then_inc(rel_in, 16)
            gp.memset(ident[:, :], 0.0).then_inc(consts, 1)
            gp.memset(ident_b[:, :], 0.0).then_inc(consts, 1)
            gp.memset(neg_tri[:, :], -1.0).then_inc(consts, 1)
            gp.memset(mask_b[:, :], NEG).then_inc(consts, 1)
            gp.memset(neg_ones[:, :], -1.0).then_inc(consts, 1)
            pool.wait_ge(consts, 5)
            for m in (ident, ident_b):
                gp.affine_select(out=m[:, :], in_=m[:, :], compare_op=ALU.not_equal, fill=1.0, base=0,
                                 pattern=[[-1, P]], channel_multiplier=1).then_inc(consts, 1)
            gp.affine_select(out=neg_tri[:, :], in_=neg_tri[:, :], compare_op=ALU.is_ge, fill=0.0, base=0,
                             pattern=[[-1, P]], channel_multiplier=1).then_inc(consts, 1)
            gp.affine_select(out=mask_b[:, :], in_=mask_b[:, :], compare_op=ALU.is_ge, fill=0.0, base=0,
                             pattern=[[-1, P]], channel_multiplier=1).then_inc(consts, 1)
            gp.memset(small[:, 156:157], 0.0).then_inc(k_stored, 1)
            gp.memset(small[:, 157:158], 0.0).then_inc(v_stored, 1)
            gp.memset(small[:, 158:159], 0.0).then_inc(mix_stored, 1)
            gp.memset(mask_c[:, :], 0.0).then_inc(consts, 1)
            pool.wait_ge(consts, CONSTS + 1)
            gp.memset(mask_c[0:64, 9 * CHUNK:10 * CHUNK], NEG).then_inc(consts, 1)
            pool.wait_ge(consts, CONSTS + 2)
            gp.memset(mask_c[64:128, 0:CHUNK], NEG).then_inc(consts, 1)
            pool.wait_ge(consts, CONSTS + 3)

            for cache, out, n in ((cache_b_k, bk_s, WINDOW), (cache_b_v, bv_s, WINDOW), (cache_c_k, ck_s, PAST), (cache_c_v, cv_s, PAST)):
                gp.dma_start(out[0, 0, 0:n - DEC].rearrange("t h d -> t (h d)"),
                             cache[0, 0, DEC:n].rearrange("t h d -> t (h d)")).then_inc(cache_moved, 16)

            def suffix_sums(i):
                base = NSTEP_A * i
                for t, (j, h, kt, c0, pos) in enumerate(A_STEPS):
                    if LAST[t]:
                        continue
                    if t:
                        pool.wait_ge(t_done, base + t)
                    if pos:
                        pool.wait_ge(r_ready, R_BEFORE[-1] * i + R_BEFORE[t])
                    wait_apart(pool, sp_ready, base + t + 1)
                    dst, s = r_buf[(pos + 1) % 2], sp_buf[t % 3]
                    if pos == 0:
                        gp.tensor_copy(dst[:, c0:BQ], s[:, c0:BQ]).then_inc(r_ready, 1)
                        continue
                    c1 = A_STEPS[t - 1][3]
                    if c0 < c1:
                        gp.tensor_copy(dst[:, c0:c1], s[:, c0:c1])
                    gp.tensor_tensor(dst[:, c1:BQ], r_buf[pos % 2][:, c1:BQ], s[:, c1:BQ], ALU.add).then_inc(r_ready, 1)

            with pool.Fori(0, NA) as i:
                suffix_sums(i)
            for tt in range(TT + 1):
                pool.wait_ge(fin_made, 2 * tt + 2)
                j = tt if tt < 4 else tt - 4
                if tt < TT:
                    gp.dma_start(y_prompt[0, P * tt:P * tt + P, :], y[:, j, :]).then_inc(y_stored, 16)
                else:
                    gp.dma_start(y_sample[0], y[0:DEC, j, :]).then_inc(y_stored, 16)
            pool.wait_ge(y_stored, 16 * (TT + 1))
            pool.wait_ge(k_stored, 32 * (NA + NB + NC) + 1)
            pool.wait_ge(v_stored, 32 * (NA + NB + NC) + 1)
            pool.wait_ge(cache_moved, 64)


def alibi_table():
    def geometric(m):
        start = 2.0 ** (-8.0 / m)
        return [start ** (i + 1) for i in range(m)]
    c = 2 ** int(np.floor(np.log2(H_B)))
    slopes = np.asarray(geometric(c) + geometric(2 * c)[0::2][:H_B - c], np.float32)
    q, k = np.arange(P)[:, None], np.arange(2 * P)[None] - P
    dc = q // CHUNK - k // CHUNK
    seen = (dc >= 0) & (dc <= WINDOW // CHUNK)
    dist = np.abs(q - k).astype(np.float32)
    return np.where(seen[None], -slopes[:, None, None] * dist[None], np.float32(NEG)).astype(np.float32)


_INS = ['x_prompt', 'x_sample', 'cache_a_k', 'cache_a_v', 'cache_b_k', 'cache_b_v', 'cache_c_k', 'cache_c_v',
        'norm_pre', 'norm_post', 'w_in', 'w_out', 'attn_sinks', 'rel_bias']
_OUTS = [(1, SEQ, D), (1, DEC, D), (1, 1, SEQ, H_A, DH), (1, 1, SEQ, H_A, DH), (1, 1, DEC, H_A, DH), (1, 1, DEC, H_A, DH),
         (1, 1, WINDOW, H_BKV, DH), (1, 1, WINDOW, H_BKV, DH), (1, 1, WINDOW, H_BKV, DH), (1, 1, WINDOW, H_BKV, DH),
         (1, 1, PAST, H_C, DH), (1, 1, PAST, H_C, DH), (1, 1, PAST, H_C, DH), (1, 1, PAST, H_C, DH)]


def kernel(**inputs):
    import concourse.bacc as _bacc
    from concourse.bass_utils import run_bass_kernel_spmd as _run

    nc = _bacc.Bacc("TRN2", target_bir_lowering=False, num_devices=1)
    arrays, args = {}, []
    for name in _INS + ['alibi']:
        a = alibi_table() if name == 'alibi' else np.ascontiguousarray(inputs[name])
        arrays[f"in_{name}_dram"] = a
        args.append(nc.dram_tensor(f"in_{name}_dram", a.shape, mybir.dt.from_np(a.dtype), kind="ExternalInput").ap())
    for i, shape in enumerate(_OUTS):
        args.append(nc.dram_tensor(f"out_{i}_dram", shape, F32, kind="ExternalOutput").ap())
    build(nc, *args)
    r = _run(nc, [arrays], core_ids=[0])
    return tuple(r.results[0][f"out_{i}_dram"] for i in range(len(_OUTS)))
```
